# Optimizing a Trainium2 kernel written in Bass

```python
import math
import jax, jax.numpy as jnp
from jax import lax
import numpy as np

D_MODEL = 1024
BATCH = 1
SEQ = 256
DEPTH = 1

MIX_WIDTH = D_MODEL
HEAD_DIM = 64
ATTN_WIDTH = MIX_WIDTH // 2
N_ATTN_HEADS = ATTN_WIDTH // HEAD_DIM
CONV_WIDTH = MIX_WIDTH - ATTN_WIDTH
CONV_GROUPS = 8
CONV_KERNEL = 31
MOBA_BLOCK = 256
MOBA_TOPK = 3
Q_CHUNK = 32
N_BUCKETS = 32
MAX_DISTANCE = 1024
FFN_HIDDEN = 2816
FFN_CONV = 3
EPS = 1e-6
NEG = -1e30

kernel_name = "hymba_moba_conformer_convffn_adaln"

def rmsnorm(x, g):
    xf = x.astype(jnp.float32)
    y = xf * lax.rsqrt(jnp.mean(xf * xf, axis=-1, keepdims=True) + EPS)
    return y.astype(x.dtype) * g

def group_norm(x, g, b, groups):
    B, S, C = x.shape
    xf = x.astype(jnp.float32).reshape(B, S, groups, C // groups)
    mu = jnp.mean(xf, axis=-1, keepdims=True)
    var = jnp.mean(jnp.square(xf - mu), axis=-1, keepdims=True)
    y = ((xf - mu) * lax.rsqrt(var + EPS)).reshape(B, S, C)
    return y.astype(x.dtype) * g + b

def causal_dwconv(x, w, b):
    K, C = w.shape
    y = lax.conv_general_dilated(
        x, w[:, None, :], window_strides=(1,), padding=[(K - 1, 0)],
        dimension_numbers=("NWC", "WIO", "NWC"), feature_group_count=C)
    return y + b

def t5_bucket(dist):
    n = jnp.maximum(dist, 0)
    max_exact = N_BUCKETS // 2
    nf = jnp.maximum(n, 1).astype(jnp.float32)
    large = max_exact + (jnp.log(nf / max_exact) / math.log(MAX_DISTANCE / max_exact)
                         * (N_BUCKETS - max_exact)).astype(jnp.int32)
    large = jnp.minimum(large, N_BUCKETS - 1)
    return jnp.where(n < max_exact, n, large)

def moba_attention(q, k, v, rel_bias):
    B, H, S, hd = q.shape
    s_pad = -(-S // MOBA_BLOCK) * MOBA_BLOCK
    pad = ((0, 0), (0, 0), (0, s_pad - S), (0, 0))
    k_p = jnp.pad(k, pad)
    v_p = jnp.pad(v, pad)
    nb = s_pad // MOBA_BLOCK
    topk = min(MOBA_TOPK, nb)
    kb = k_p.reshape(B, H, nb, MOBA_BLOCK, hd)
    vb = v_p.reshape(B, H, nb, MOBA_BLOCK, hd)
    kmean = jnp.mean(kb, axis=3)
    scale = hd ** -0.5
    b_idx = jnp.arange(B)[:, None, None, None]
    h_idx = jnp.arange(H)[None, :, None, None]
    h_idx5 = jnp.arange(H)[None, :, None, None, None]
    offs = jnp.arange(MOBA_BLOCK)
    n_chunks = S // Q_CHUNK

    def chunk(ci):
        q0 = ci * Q_CHUNK
        ib = q0 // MOBA_BLOCK
        qc = lax.dynamic_slice_in_dim(q, q0, Q_CHUNK, axis=2)
        qpos = q0 + jnp.arange(Q_CHUNK)
        gate = jnp.einsum("bhqd,bhnd->bhqn", qc, kmean).astype(jnp.float32)
        gate = jnp.where(jnp.arange(nb) < ib, gate, -jnp.inf)
        _, idx = lax.top_k(gate, topk)
        valid = jnp.arange(topk) < ib
        k_sel = kb[b_idx, h_idx, idx]
        v_sel = vb[b_idx, h_idx, idx]
        s_sel = jnp.einsum("bhqd,bhqnkd->bhqnk", qc, k_sel).astype(jnp.float32) * scale
        kpos_sel = idx[..., None] * MOBA_BLOCK + offs
        bucket_sel = t5_bucket(qpos[None, None, :, None, None] - kpos_sel)
        s_sel = s_sel + rel_bias[h_idx5, bucket_sel].astype(jnp.float32)
        s_sel = jnp.where(valid[:, None], s_sel, NEG)
        k_own = lax.dynamic_slice_in_dim(k_p, ib * MOBA_BLOCK, MOBA_BLOCK, axis=2)
        v_own = lax.dynamic_slice_in_dim(v_p, ib * MOBA_BLOCK, MOBA_BLOCK, axis=2)
        s_own = jnp.einsum("bhqd,bhkd->bhqk", qc, k_own).astype(jnp.float32) * scale
        d_own = qpos[:, None] - (ib * MOBA_BLOCK + offs)[None, :]
        s_own = s_own + rel_bias[:, t5_bucket(d_own)][None].astype(jnp.float32)
        s_own = jnp.where(d_own >= 0, s_own, NEG)
        s_all = jnp.concatenate(
            [s_sel.reshape(B, H, Q_CHUNK, topk * MOBA_BLOCK), s_own], axis=-1)
        p = jax.nn.softmax(s_all, axis=-1).astype(v.dtype)
        p_sel = p[..., :topk * MOBA_BLOCK].reshape(B, H, Q_CHUNK, topk, MOBA_BLOCK)
        p_own = p[..., topk * MOBA_BLOCK:]
        return (jnp.einsum("bhqnk,bhqnkd->bhqd", p_sel, v_sel)
                + jnp.einsum("bhqk,bhkd->bhqd", p_own, v_own))

    out = lax.map(chunk, jnp.arange(n_chunks))
    return out.transpose(1, 0, 3, 2, 4).reshape(B, S, H, hd)

def setup_inputs(seed: int = 0) -> dict:
    key = jax.random.key(seed)
    ks = jax.random.split(key, 20)
    D, F = D_MODEL, FFN_HIDDEN
    n_in = 3 * ATTN_WIDTH + 2 * CONV_WIDTH
    nrm = jax.random.normal
    f32 = jnp.float32
    return {
        "x": nrm(ks[0], (BATCH, SEQ, D), f32),
        "c": nrm(ks[1], (BATCH, D), f32),
        "rel_bias": 0.5 * nrm(ks[2], (N_ATTN_HEADS, N_BUCKETS), f32),
        "ada_w": 0.5 * D ** -0.5 * nrm(ks[3], (DEPTH, D, 6 * D), f32),
        "ada_b": 0.02 * nrm(ks[4], (DEPTH, 6 * D), f32),
        "norm1_g": 1.0 + 0.05 * nrm(ks[5], (DEPTH, D), f32),
        "w_in": D ** -0.5 * nrm(ks[6], (DEPTH, D, n_in), f32),
        "q_norm_g": 1.0 + 0.05 * nrm(ks[7], (DEPTH, HEAD_DIM), f32),
        "k_norm_g": 1.0 + 0.05 * nrm(ks[8], (DEPTH, HEAD_DIM), f32),
        "conv_dw_w": CONV_KERNEL ** -0.5 * nrm(ks[9], (DEPTH, CONV_KERNEL, CONV_WIDTH), f32),
        "conv_dw_b": 0.02 * nrm(ks[10], (DEPTH, CONV_WIDTH), f32),
        "conv_norm_g": 1.0 + 0.05 * nrm(ks[11], (DEPTH, CONV_WIDTH), f32),
        "conv_norm_b": 0.02 * nrm(ks[12], (DEPTH, CONV_WIDTH), f32),
        "w_out": MIX_WIDTH ** -0.5 * nrm(ks[13], (DEPTH, MIX_WIDTH, D), f32),
        "norm2_g": 1.0 + 0.05 * nrm(ks[14], (DEPTH, D), f32),
        "w_up": D ** -0.5 * nrm(ks[15], (DEPTH, D, 2 * F), f32),
        "ffn_dw_w": FFN_CONV ** -0.5 * nrm(ks[16], (DEPTH, FFN_CONV, 2 * F), f32),
        "ffn_dw_b": 0.02 * nrm(ks[17], (DEPTH, 2 * F), f32),
        "w_down": F ** -0.5 * nrm(ks[18], (DEPTH, F, D), f32),
    }

def reference(x, c, rel_bias, ada_w, ada_b, norm1_g, w_in, q_norm_g, k_norm_g,
              conv_dw_w, conv_dw_b, conv_norm_g, conv_norm_b, w_out, norm2_g,
              w_up, ffn_dw_w, ffn_dw_b, w_down):
    B, S, D = x.shape
    H, hd = N_ATTN_HEADS, HEAD_DIM
    sc = jax.nn.silu(c)
    for l in range(DEPTH):
        mod = sc @ ada_w[l] + ada_b[l]
        sh1, sc1, g1, sh2, sc2, g2 = [m[:, None, :] for m in jnp.split(mod, 6, axis=-1)]

        xn = rmsnorm(x, norm1_g[l]) * (1.0 + sc1) + sh1
        proj = xn @ w_in[l]
        q, k, v, ca, cg = jnp.split(
            proj, np.cumsum([ATTN_WIDTH] * 3 + [CONV_WIDTH]).tolist(), axis=-1)
        q = rmsnorm(q.reshape(B, S, H, hd), q_norm_g[l]).transpose(0, 2, 1, 3)
        k = rmsnorm(k.reshape(B, S, H, hd), k_norm_g[l]).transpose(0, 2, 1, 3)
        v = v.reshape(B, S, H, hd).transpose(0, 2, 1, 3)
        y_attn = moba_attention(q, k, v, rel_bias).reshape(B, S, ATTN_WIDTH)

        a = ca * jax.nn.sigmoid(cg)
        a = causal_dwconv(a, conv_dw_w[l], conv_dw_b[l])
        a = jax.nn.silu(group_norm(a, conv_norm_g[l], conv_norm_b[l], CONV_GROUPS))

        y_mix = jnp.concatenate([y_attn, a], axis=-1) @ w_out[l]
        x = x + g1 * y_mix

        xn2 = rmsnorm(x, norm2_g[l]) * (1.0 + sc2) + sh2
        h = causal_dwconv(xn2 @ w_up[l], ffn_dw_w[l], ffn_dw_b[l])
        u, g = jnp.split(h, 2, axis=-1)
        x = x + g2 * ((jax.nn.silu(g) * u) @ w_down[l])
    return x


_drawn_inputs = setup_inputs


def setup_inputs(seed=0):
    import zlib

    import numpy as np

    out = dict(_drawn_inputs(seed))
    spreads = {}
    factors = {'rel_bias': 2.933,
     'ada_b': 2.775,
     'norm1_g': 6.585,
     'q_norm_g': 8.0,
     'k_norm_g': 8.0,
     'conv_dw_b': 8.0,
     'conv_norm_g': 7.189,
     'conv_norm_b': 29.733,
     'norm2_g': 3.757,
     'ffn_dw_b': 8.0}
    for name, (base, spread) in spreads.items():
        noise = np.random.default_rng([zlib.crc32(name.encode()), seed]).standard_normal(out[name].shape)
        drawn = base * np.exp(spread * noise) if base else spread * noise
        out[name] = __import__('jax').numpy.asarray(drawn.astype(out[name].dtype))
    for name, factor in factors.items():
        out[name] = (out[name] * factor).astype(out[name].dtype)
    return out
```

```python
import math
from contextlib import ExitStack

import numpy as np

import concourse.bass as bass
from concourse import mybir

D_MODEL, SEQ = 1024, 256
HEADS, HEAD_DIM = 8, 64
CONV_TAPS, FFN_TAPS = 31, 3
FFN_HIDDEN = 2816
N_BUCKETS, MAX_DISTANCE = 32, 1024
EPS, NEG = 1e-6, -1e30

P = 128
KT = D_MODEL // P
ST = SEQ // P
CT = D_MODEL // 2 // P
FT = FFN_HIDDEN // P
SLOT = 2048

ADA_GROUPS = [(0, 1, 2, 3), (4, 5, 10, 11), (6, 7, 8, 9)]
UP_DOWN = [("up", 0), ("up", 1)]
for _i in range(FT // 2):
    if _i + 1 < FT // 2:
        UP_DOWN += [("up", 2 * _i + 2), ("up", 2 * _i + 3)]
    UP_DOWN += [("down", _i)]
STREAM = ([("ada", k) for k in range(KT - 1)] + [("conv", 0), ("ada", KT - 1)]
          + [("conv", j) for j in range(1, CT)] + [("qk", j) for j in range(CT)] + [("v", 0), ("v", 1)]
          + [("out", j) for j in range(3)] + [("ada", KT + k) for k in range(2 * KT)] + [("out", 3)] + UP_DOWN)
SPLIT = [x for x in STREAM if x[0] != "ada"]
AT = {x: n for n, x in enumerate(STREAM)}
SP_AT = {x: m for m, x in enumerate(SPLIT)}
RAW, PARTS = 6, 3

COLS = {}
_at = 0
for _name, _n in [("c", KT), ("norm1_g", KT), ("norm2_g", KT), ("sh1_b", KT), ("sc1_b", KT), ("sh2_b", KT),
                  ("sc2_b", KT), ("conv_w", CT * CONV_TAPS), ("conv_b", CT), ("gn_g", CT), ("gn_b", CT),
                  ("ffn_w", 2 * FT * FFN_TAPS), ("ffn_b", 2 * FT), ("q_g", 1), ("k_g", 1)]:
    COLS[_name] = (_at, _n)
    _at += _n
N_COLS = _at

CONV_PER_STEP, CONV_PER_HEAD = 6, 6


def bucket_ranges():
    d = np.arange(SEQ)
    exact = N_BUCKETS // 2
    nf = np.maximum(d, 1).astype(np.float32)
    large = exact + (np.log(nf / np.float32(exact)) / np.float32(math.log(MAX_DISTANCE / exact))
                     * np.float32(N_BUCKETS - exact)).astype(np.int32)
    b = np.where(d < exact, d, np.minimum(large, N_BUCKETS - 1))
    return [(int(v), int(d[b == v][0]), int(d[b == v][-1])) for v in np.unique(b)]


def hymba_layer(nc, stream, x_t, x_rows, cols_in, ada_b_gates, rel_bias, out):
    f32, f32r = mybir.dt.float32, mybir.dt.float32r
    ALU, ACT = mybir.AluOpType, mybir.ActivationFunctionType

    toeplitz_rows = nc.dram_tensor("toeplitz_rows", [HEADS, 384], f32, kind="Internal").ap()

    ctx = ExitStack()
    with ctx:
        def sb(name, shape, dt=f32):
            return ctx.enter_context(nc.sbuf_tensor(name, shape, dt))

        def sem(name):
            return ctx.enter_context(nc.semaphore(name))

        bank = [ctx.enter_context(nc.psum_tensor(f"bank{i}", [P, 512], f32)) for i in range(8)]

        raw = sb("raw", [P, RAW, SLOT])
        w_hi = sb("w_hi", [P, PARTS, SLOT], f32r)
        w_lo = sb("w_lo", [P, PARTS, SLOT], f32r)
        xt = sb("xt", [P, KT, SEQ])
        xmod = sb("xmod", [P, KT, SEQ])
        act_hi = sb("act_hi", [P, KT, SEQ], f32r)
        act_lo = sb("act_lo", [P, KT, SEQ], f32r)
        xr = sb("xr", [P, ST, D_MODEL])
        gate = sb("gate", [P, 2, D_MODEL])
        cols = sb("cols", [P, N_COLS])
        silu_c = sb("silu_c", [P, KT])
        gates_b = sb("gates_b", [P, 512])
        mod_rows = sb("mod_rows", [P, 512])
        scale = sb("scale", [P, 2, KT])
        shift = sb("shift", [P, 2, KT])
        rms = sb("rms", [P, SEQ])
        rinv = sb("rinv", [P, SEQ])
        ident = sb("ident", [P, P])
        ones = sb("ones", [P, P])
        half_mean = sb("half_mean", [P, P])
        to_group = sb("to_group", [P, 8, 16])
        from_group = sb("from_group", [16, 8, P])
        table = sb("table", [HEADS, N_BUCKETS])
        bias_rows = sb("bias_rows", [HEADS, 384])
        bias = sb("bias", [P, HEADS, SEQ])
        glu_gate = sb("glu_gate", [P, 2, SEQ])
        glu = sb("glu", [P, CT, SEQ + CONV_TAPS - 1])
        conv = sb("conv", [P, CT, SEQ])
        gn_stat = sb("gn_stat", [4, 2, SEQ])
        gn_rstd = sb("gn_rstd", [4, 2, SEQ])
        qk = sb("qk", [P, CT, 2 * SEQ])
        qk_sq = gate[:, 0, :].rearrange("p (a b) -> p a b", a=2)
        qk_stat = sb("qk_stat", [16, SEQ])
        qk_rstd = sb("qk_rstd", [16, SEQ])
        q_gain = sb("q_gain", [P, 1])
        v = gate[:, 1, :].rearrange("p (t n) -> p t n", t=ST)
        prob = sb("prob", [P, 3, 384])
        prob_t = sb("prob_t", [P, 2, 384])
        peak = sb("peak", [P, 2 * HEADS])
        npeak = sb("npeak", [P, 2 * HEADS])
        total = sb("total", [P, 2 * HEADS])
        rtotal = sb("rtotal", [P, 2 * HEADS])
        ssq2 = sb("ssq2", [P, ST])
        rms2 = sb("rms2", [P, ST])
        rinv2 = sb("rinv2", [P, ST])
        tmp = qk
        ug = bias[:, 0:4, :].rearrange("p (t g) s -> p t g s", t=2)
        silu_g = bias[:, 4:6, :]
        hid = bias[:, 6:8, :]
        hid_hi = sb("hid_hi", [P, 4, SEQ], f32r)
        hid_lo = sb("hid_lo", [P, 4, SEQ], f32r)
        eps = sb("eps", [P, 1])

        raw_ready = [sem(f"raw_ready{i}") for i in range(RAW)]
        cols_ready, xt_ready, xr_ready = sem("cols_ready"), sem("xt_ready"), sem("xr_ready")
        gates_b_ready, table_ready = sem("gates_b_ready"), sem("table_ready")
        rows_stored, bias_ready = sem("rows_stored"), sem("bias_ready")
        pool_step, consts_ready = sem("pool_step"), sem("consts_ready")
        ada_used, w_used = sem("ada_used"), sem("w_used")
        hi_done, lo_done = sem("hi_done"), sem("lo_done")
        silu_c_ready, xsq_ready, ssq_ready, rms_ready = (sem(s) for s in ("silu_c_ready", "xsq_ready", "ssq_ready", "rms_ready"))
        mod_done, mod_rows_ready, mod_cols_ready = sem("mod_done"), sem("mod_rows_ready"), sem("mod_cols_ready")
        mod_cols_read = sem("mod_cols_read")
        gate_bc, gate_ready = sem("gate_bc"), sem("gate_ready")
        xn_full, xn_hi, xn_lo = sem("xn_full"), sem("xn_hi"), sem("xn_lo")
        sig_ready, glu_ready = sem("sig_ready"), sem("glu_ready")
        tap = sem("tap")
        qk_raw, qk_sq_ready, qk_ssq, qk_std, qk_rs, qk_bc, qk_normed = (
            sem(s) for s in ("qk_raw", "qk_sq_ready", "qk_ssq", "qk_std", "qk_rs", "qk_bc", "qk_normed"))
        v_ready, rinv_ready, xhat_ready, mixed = sem("v_ready"), sem("rinv_ready"), sem("xhat_ready"), sem("mixed")
        scores, biased, peaked, exped, inverted, normed, turned, turned_copied, attended, att_hi, att_lo = (
            sem(s) for s in ("scores", "biased", "peaked", "exped", "inverted", "normed", "turned", "turned_copied",
                             "attended", "att_hi", "att_lo"))
        gn_mean, gn_centred, gn_sq, gn_ssq, gn_std, gn_rs, gn_bc, gn_scaled, gn_silu, mix_hi, mix_lo = (
            sem(s) for s in ("gn_mean", "gn_centred", "gn_sq", "gn_ssq", "gn_std", "gn_rs", "gn_bc", "gn_scaled",
                             "gn_silu", "mix_hi", "mix_lo"))
        x2_part, x2_ready, x2_sq, x2_std, x2_rs, x2_normed, x2_turned, xn2_full, xn2_hi, xn2_lo = (
            sem(s) for s in ("x2_part", "x2_ready", "x2_sq", "x2_std", "x2_rs", "x2_normed", "x2_turned", "xn2_full",
                             "xn2_hi", "xn2_lo"))
        tap2, tap1, tap0, gated, hidden, hid_hi_ready, hid_lo_ready, down_done = (
            sem(s) for s in ("tap2", "tap1", "tap0", "gated", "hidden", "hid_hi_ready", "hid_lo_ready", "down_done"))
        out_part, out_ready, stored = sem("out_part"), sem("out_ready"), sem("stored")

        def col(name, i=0):
            a, _ = COLS[name]
            return cols[:, a + i:a + i + 1]

        def cols_of(name):
            a, n = COLS[name]
            return cols[:, a:a + n]

        def slot(kind, i):
            return raw[:, AT[kind, i] % RAW, :]

        def arrived(eng, kind, i):
            n = AT[kind, i]
            eng.wait_ge(raw_ready[n % RAW], 16 * (n // RAW + 1))

        def parts(m):
            return w_hi[:, m % PARTS, :], w_lo[:, m % PARTS, :]

        ROWS = [(0, P, P), (P, 384, 0)]
        GN_BANK = (4, 6)
        TAPS = [(2 * pair + t, i) for pair in range(CT // 2) for i in range(CONV_TAPS) for t in range(2)]

        block = ctx.enter_context(nc.Block())

        @block.sync
        def _(sp):
            sp.dma_start(cols[:, :], cols_in).then_inc(cols_ready, 16)
            for n, (kind, i) in enumerate(STREAM):
                if n >= RAW:
                    k0, i0 = STREAM[n - RAW]
                    if k0 == "ada":
                        sp.wait_ge(ada_used, i0 + 1)
                    else:
                        sp.wait_ge(lo_done, SP_AT[k0, i0] + 1)
                sp.dma_start(raw[:, n % RAW, :], stream[n]).then_inc(raw_ready[n % RAW], 16)
                if n == 0:
                    sp.dma_start(xt[:, :, :], x_t).then_inc(xt_ready, 16)
                if (kind, i) == ("qk", 1):
                    sp.dma_start(gates_b[:, :], ada_b_gates).then_inc(gates_b_ready, 16)
                    sp.dma_start(xr[:, :, :], x_rows).then_inc(xr_ready, 16)
            for t in range(ST):
                for n in range(2):
                    sp.wait_ge(out_ready, 2 * t + n + 1)
                    sp.dma_start(out[t, :, n * 512:(n + 1) * 512], xmod[:, 4 * t + 2 * n:4 * t + 2 * n + 2, :].rearrange("p a b -> p (a b)")).then_inc(stored, 16)
            sp.wait_ge(stored, 16 * 2 * ST)

        @block.gpsimd
        def _(pool):
            step = [0]

            def chained(ins):
                step[0] += 1
                ins.then_inc(pool_step, 1)
                pool.wait_ge(pool_step, step[0])

            pool.dma_start(table[:, :], rel_bias).then_inc(table_ready, 16)
            chained(nc.gpsimd.memset(eps[:, :], EPS))
            chained(nc.gpsimd.memset(ones[:, :], 1.0))
            chained(nc.gpsimd.memset(half_mean[:, :], 0.0))
            chained(nc.gpsimd.memset(glu[:, :, 0:CONV_TAPS - 1], 0.0))
            chained(nc.gpsimd.memset(from_group[:, :, :], 0.0))
            chained(nc.gpsimd.memset(to_group[:, :, :], 0.0))
            chained(nc.gpsimd.memset(ident[:, :], 0.0))
            flat = to_group[:, :, :].rearrange("p j m -> p (j m)")
            for half in range(2):
                rows = slice(64 * half, 64 * half + 64)
                chained(nc.gpsimd.memset(flat[rows, half:128:18], 1.0))
                chained(nc.gpsimd.memset(half_mean[rows, rows], 1.0 / 64))
            chained(nc.gpsimd.affine_select(out=ident[:, :], in_=ident[:, :], compare_op=ALU.not_equal, fill=1.0,
                                            base=0, pattern=[[-1, P]], channel_multiplier=1))
            wide = from_group[:, :, :].rearrange("p j (a c) -> p j a c", a=2)
            nc.gpsimd.affine_select(out=wide, in_=wide, compare_op=ALU.not_equal, fill=1.0, base=0,
                                    pattern=[[-2, 8], [-1, 2], [0, 64]], channel_multiplier=1).then_inc(consts_ready, 1)
            pool.wait_ge(table_ready, 16)
            chained(nc.gpsimd.memset(bias_rows[:, 0:P - 1], NEG))
            chained(nc.gpsimd.memset(bias_rows[:, 383:384], NEG))
            for b, lo, hi in bucket_ranges():
                n = hi - lo + 1
                chained(nc.gpsimd.tensor_copy(bias_rows[:, P - 1 + lo:P + hi],
                                              table[:, b:b + 1].to_broadcast([HEADS, n])))
            pool.dma_start(toeplitz_rows, bias_rows[:, :]).then_inc(rows_stored, 16)
            pool.wait_ge(rows_stored, 16)
            pool.wait_ge(w_used, 1)
            pool.dma_start(bias[:, :, :], bass.AP(toeplitz_rows.tensor, 0, [[1, P], [384, HEADS], [1, SEQ]])
                           ).then_inc(bias_ready, 16)

        @block.scalar
        def _(act):
            def split_hi(m):
                if m >= len(SPLIT):
                    return
                arrived(act, *SPLIT[m])
                if m >= PARTS:
                    act.wait_ge(w_used, m - PARTS + 1)
                nc.scalar.activation(w_hi[:, m % PARTS, :], slot(*SPLIT[m]), ACT.Copy).then_inc(hi_done, 1)

            act.wait_ge(cols_ready, 16)
            nc.scalar.activation(silu_c[:, :], cols_of("c"), ACT.Silu).then_inc(silu_c_ready, 1)
            act.wait_ge(xt_ready, 16)
            nc.scalar.activation(xmod[:, :, :], xt[:, :, :], ACT.Square).then_inc(xsq_ready, 1)
            act.wait_ge(consts_ready, 1)
            act.wait_ge(ssq_ready, 1)
            nc.scalar.activation(rms[:, :], bank[7][:, 0:SEQ], ACT.Sqrt, scale=1.0 / D_MODEL,
                                 bias=eps[:, :]).then_inc(rms_ready, 1)
            split_hi(0)
            act.wait_ge(xhat_ready, 1)
            act.wait_ge(mod_cols_read, 2)
            for k in range(KT):
                nc.scalar.activation(act_hi[:, k, :], xt[:, k, :], ACT.Identity, scale=scale[:, 0, k:k + 1],
                                     bias=shift[:, 0, k:k + 1]).then_inc(xn_hi, 1)
            split_hi(1)

            def conv_gate(j):
                act.wait_ge(w_used, SP_AT["conv", j] + 1)
                if j >= 2:
                    act.wait_ge(glu_ready, j - 1)
                nc.scalar.activation(glu_gate[:, j % 2, :], bank[j % 2][:, 0:SEQ], ACT.Sigmoid).then_inc(sig_ready, 1)

            def qk_raw_out(j):
                act.wait_ge(w_used, SP_AT["qk", j] + 1)
                nc.scalar.activation(qk[:, j, :], bank[j % 2][:, :], ACT.Copy).then_inc(qk_raw, 1)
                if j >= 2:
                    act.wait_ge(qk_ssq, j - 1)
                nc.scalar.activation(qk_sq[:, j % 2, :], bank[j % 2][:, :], ACT.Square).then_inc(qk_sq_ready, 1)

            def after(m):
                kind, i = SPLIT[m]
                if kind == "conv":
                    conv_gate(i)
                elif kind == "qk":
                    qk_raw_out(i)
                    if i == CT - 1:
                        act.wait_ge(qk_ssq, CT)
                        nc.scalar.activation(qk_stat[:, :], bank[6][0:16, 0:SEQ], ACT.Sqrt, scale=1.0 / HEAD_DIM,
                                             bias=eps[0:16, :]).then_inc(qk_std, 1)

            for m in range(SP_AT["v", 1] + 1):
                split_hi(m + 2)
                if m >= 1:
                    after(m - 1)
            act.wait_ge(w_used, SP_AT["v", 1] + 1)
            for t in range(ST):
                nc.scalar.activation(v[:, t, :], bank[4 + t][:, :], ACT.Copy).then_inc(v_ready, 1)

            def exps(h):
                for t, (a, b, _) in enumerate(ROWS):
                    n = 2 * h + t
                    act.wait_ge(peaked, h + 1)
                    nc.scalar.activation(prob[:, h % 3, a:b], prob[:, h % 3, a:b], ACT.Exp, bias=npeak[:, n:n + 1],
                                         accum_out=total[:, n:n + 1]).then_inc(exped, 1)

            def normalise(h):
                act.wait_ge(inverted, h + 1)
                for t, (a, b, _) in enumerate(ROWS):
                    n = 2 * h + t
                    last = nc.scalar.activation(prob[:, h % 3, a:b], prob[:, h % 3, a:b], ACT.Copy,
                                                scale=rtotal[:, n:n + 1])
                last.then_inc(normed, 1)

            def turn_copy(h):
                act.wait_ge(turned, h + 1)
                if h >= 2:
                    act.wait_ge(attended, h - 1)
                nc.scalar.activation(prob_t[:, h % 2, :], bank[3 + h % 2][:, 0:384], ACT.Copy).then_inc(turned_copied, 1)

            def att_hi_part(j):
                act.wait_ge(attended, 2 * j + 2)
                nc.scalar.activation(act_hi[:, j, :], bank[6][:, 0:SEQ], ACT.Copy).then_inc(att_hi, 1)

            for h in range(HEADS + 1):
                if h < HEADS:
                    exps(h)
                if h == 1:
                    split_hi(SP_AT["out", 2])
                if h >= 1:
                    normalise(h - 1)
                    turn_copy(h - 1)
                    if h % 2 == 1 and h >= 3:
                        att_hi_part((h - 3) // 2)
            att_hi_part(CT - 1)
            def gn_square(g):
                act.wait_ge(gn_centred, g + 1)
                nc.scalar.activation(xmod[:, 2 * g:2 * g + 2, :], conv[:, 2 * g:2 * g + 2, :], ACT.Square).then_inc(gn_sq, 1)
                act.wait_ge(gn_ssq, g + 1)
                nc.scalar.activation(gn_stat[:, g, :], bank[7][0:4, 0:SEQ], ACT.Sqrt, scale=1.0 / 64,
                                     bias=eps[0:4, :]).then_inc(gn_std, 1)

            def gn_swish(g):
                for j in (2 * g, 2 * g + 1):
                    act.wait_ge(gn_scaled, j + 1)
                    nc.scalar.activation(xmod[:, CT + j, :], conv[:, j, :], ACT.Silu, bias=col("gn_b", j)).then_inc(gn_silu, 1)
                for j in (2 * g, 2 * g + 1):
                    act.wait_ge(gn_silu, j + 1)
                    nc.scalar.activation(act_hi[:, CT + j, :], xmod[:, CT + j, :], ACT.Copy).then_inc(mix_hi, 1)

            def gate_out(n):
                act.wait_ge(gate_bc, n + 1)
                nc.scalar.activation(gate[:, n // 2, (n % 2) * 512:(n % 2) * 512 + 512], bank[4 + n % 2][:, :],
                                     ACT.Copy).then_inc(gate_ready, 1)

            gn_square(0)
            split_hi(SP_AT["out", 3])
            gn_swish(0)
            gn_square(1)
            gate_out(0)
            gate_out(1)
            split_hi(SP_AT["up", 0])
            gn_swish(1)
            gate_out(2)
            gate_out(3)
            split_hi(SP_AT["up", 1])
            for t in range(ST):
                act.wait_ge(x2_ready, 2 * t + 2)
                nc.scalar.activation(xmod[:, 4 * t:4 * t + 4, :].rearrange("p a b -> p (a b)"), xr[:, t, :],
                                     ACT.Square, accum_out=ssq2[:, t:t + 1]).then_inc(x2_sq, 1)
            act.wait_ge(x2_sq, ST)
            nc.scalar.activation(rms2[:, :], ssq2[:, :], ACT.Sqrt, scale=1.0 / D_MODEL, bias=eps[:, :]).then_inc(x2_std, 1)
            for k in range(KT):
                act.wait_ge(xn2_full, k + 1)
                nc.scalar.activation(act_hi[:, k, :], xt[:, k, :], ACT.Copy).then_inc(xn2_hi, 1)

            def tap_two(t):
                act.wait_ge(w_used, SP_AT["up", t] + 1)
                if t >= 2:
                    act.wait_ge(hidden, t - 1)
                for g in range(2):
                    nc.scalar.activation(ug[:, t % 2, g, :], bank[4 + 2 * (t % 2) + g][:, 0:SEQ], ACT.Identity,
                                         scale=col("ffn_w", (g * FT + t) * FFN_TAPS + 2),
                                         bias=col("ffn_b", g * FT + t)).then_inc(tap2, 1)

            def gate_silu(t):
                act.wait_ge(tap0, 2 * t + 2)
                nc.scalar.activation(silu_g[:, t % 2, :], ug[:, t % 2, 1, :], ACT.Silu).then_inc(gated, 1)

            def hid_high(t):
                act.wait_ge(hidden, t + 1)
                if t >= 4:
                    act.wait_ge(w_used, SP_AT["down", t // 2 - 2] + 1)
                nc.scalar.activation(hid_hi[:, t % 4, :], hid[:, t % 2, :], ACT.Copy).then_inc(hid_hi_ready, 1)

            def after_up(t):
                tap_two(t)
                gate_silu(t)
                hid_high(t)

            m0 = SP_AT["up", 0]
            for m in range(m0, len(SPLIT)):
                split_hi(m + 2)
                if m > m0 and SPLIT[m - 1][0] == "up":
                    after_up(SPLIT[m - 1][1])

        @block.vector
        def _(dve):
            def split_lo(m):
                if m >= len(SPLIT):
                    return
                dve.wait_ge(hi_done, m + 1)
                arrived(dve, *SPLIT[m])
                if m >= PARTS:
                    dve.wait_ge(w_used, m - PARTS + 1)
                nc.vector.tensor_tensor(w_lo[:, m % PARTS, :], slot(*SPLIT[m]),
                                        w_hi[:, m % PARTS, :].bitcast(f32), ALU.subtract).then_inc(lo_done, 1)

            dve.wait_ge(rms_ready, 1)
            nc.vector.reciprocal(rinv[:, :], rms[:, :]).then_inc(rinv_ready, 1)
            dve.wait_ge(rinv_ready, 1)
            dve.wait_ge(xt_ready, 16)
            for k in range(KT):
                last = nc.vector.tensor_tensor(xt[:, k, :], xt[:, k, :], rinv[:, :], ALU.mult)
            last.then_inc(xhat_ready, 1)
            nc.vector.tensor_scalar(q_gain[:, :], col("q_g"), HEAD_DIM ** -0.5, None, ALU.mult)

            def xn_low(k):
                dve.wait_ge(xn_full, k + 1)
                dve.wait_ge(xn_hi, k + 1)
                nc.vector.tensor_tensor(act_lo[:, k, :], xmod[:, k, :], act_hi[:, k, :].bitcast(f32),
                                        ALU.subtract).then_inc(xn_lo, 1)

            def mod_columns(which, gain, shift_b, scale_b):
                dve.wait_ge(mod_done, 1 + 2 * which)
                nc.vector.tensor_copy(mod_rows[:, :], bank[0 if which == 0 else 5][:, :]).then_inc(mod_rows_ready, 1)
                dve.wait_ge(mod_cols_ready, which + 1)
                turned_rows = bank[1 if which == 0 else 5][:, :].rearrange("p (j q r) -> p q j r", j=4, q=4)
                nc.vector.tensor_tensor(shift[:, which, :].rearrange("p (q j) -> p q j", q=2), turned_rows[:, 0:2, :, 0],
                                        cols_of(shift_b).rearrange("p (q j) -> p q j", q=2), ALU.add)
                nc.vector.tensor_tensor(scale[:, which, :].rearrange("p (q j) -> p q j", q=2), turned_rows[:, 2:4, :, 0],
                                        cols_of(scale_b).rearrange("p (q j) -> p q j", q=2), ALU.add).then_inc(mod_cols_read, 1)
                dve.wait_ge(mod_cols_read, 2 * which + 1)
                nc.vector.scalar_tensor_tensor(scale[:, which, :], scale[:, which, :], 1.0, cols_of(gain), ALU.add,
                                               ALU.mult).then_inc(mod_cols_read, 1)
                dve.wait_ge(mod_cols_read, 2 * which + 2)

            split_lo(0)
            mod_columns(0, "norm1_g", "sh1_b", "sc1_b")
            dve.wait_ge(xhat_ready, 1)
            for k in range(KT):
                nc.vector.tensor_scalar(xmod[:, k, :], xt[:, k, :], scale[:, 0, k:k + 1], shift[:, 0, k:k + 1],
                                        ALU.mult, ALU.add).then_inc(xn_full, 1)
                if k >= 1:
                    xn_low(k - 1)
            xn_low(KT - 1)
            split_lo(1)

            done_taps = [0]

            def taps(n):
                for n_tap in range(done_taps[0], min(done_taps[0] + n, len(TAPS))):
                    j, i = TAPS[n_tap]
                    w = col("conv_w", j * CONV_TAPS + i)
                    if i == 0:
                        dve.wait_ge(glu_ready, j + 1)
                        nc.vector.tensor_scalar(conv[:, j, :], glu[:, j, 0:SEQ], w, col("conv_b", j), ALU.mult,
                                                ALU.add).then_inc(tap, 1)
                    else:
                        dve.wait_ge(tap, n_tap - 1)
                        nc.vector.scalar_tensor_tensor(conv[:, j, :], glu[:, j, i:i + SEQ], w, conv[:, j, :],
                                                       ALU.mult, ALU.add).then_inc(tap, 1)
                    done_taps[0] = n_tap + 1

            def after(m):
                kind, j = SPLIT[m]
                if kind == "conv":
                    dve.wait_ge(sig_ready, j + 1)
                    nc.vector.tensor_tensor(glu[:, j, CONV_TAPS - 1:], bank[j % 2][:, SEQ:2 * SEQ],
                                            glu_gate[:, j % 2, :], ALU.mult).then_inc(glu_ready, 1)

            dve.wait_ge(consts_ready, 1)
            for m in range(SP_AT["v", 1] + 1):
                split_lo(m + 2)
                if m >= 1:
                    after(m - 1)
                if m >= 2:
                    taps(CONV_PER_STEP)
            dve.wait_ge(qk_std, 1)
            nc.vector.reciprocal(qk_rstd[:, :], qk_stat[:, :]).then_inc(qk_rs, 1)
            for j in range(CT):
                dve.wait_ge(qk_bc, j + 1)
                dve.wait_ge(qk_raw, j + 1)
                for part, gain in enumerate((q_gain[:, :], col("k_g"))):
                    cut = slice(part * SEQ, (part + 1) * SEQ)
                    nc.vector.scalar_tensor_tensor(qk[:, j, cut], qk[:, j, cut], gain, bank[j % 2][:, cut], ALU.mult,
                                                   ALU.mult).then_inc(qk_normed, 1)

            def add_bias(h):
                dve.wait_ge(scores, h + 1)
                if h >= 3:
                    dve.wait_ge(turned, h - 2)
                for t, (a, b, c) in enumerate(ROWS):
                    n = 2 * h + t
                    nc.vector.tensor_tensor_reduce(prob[:, h % 3, a:b], bank[h % 3][:, a:b], bias[:, h, SEQ - 1 - c::-1],
                                                   1.0, 2 * NEG, ALU.add, ALU.max, peak[:, n:n + 1]).then_inc(biased, 1)
                dve.wait_ge(biased, 2 * h + 2)
                nc.vector.tensor_scalar(npeak[:, 2 * h:2 * h + 2], peak[:, 2 * h:2 * h + 2], -1.0, None,
                                        ALU.mult).then_inc(peaked, 1)

            def invert(h):
                dve.wait_ge(exped, 2 * h + 2)
                nc.vector.reciprocal(rtotal[:, 2 * h:2 * h + 2], total[:, 2 * h:2 * h + 2]).then_inc(inverted, 1)

            def att_lo_part(j):
                dve.wait_ge(att_hi, j + 1)
                nc.vector.tensor_tensor(act_lo[:, j, :], bank[6][:, 0:SEQ], act_hi[:, j, :].bitcast(f32),
                                        ALU.subtract).then_inc(att_lo, 1)

            dve.wait_ge(bias_ready, 16)
            for h in range(HEADS + 1):
                if h < HEADS:
                    add_bias(h)
                if h >= 1:
                    invert(h - 1)
                if h == 2:
                    split_lo(SP_AT["out", 2])
                taps(CONV_PER_HEAD)
                if h % 2 == 1 and h >= 3:
                    att_lo_part((h - 3) // 2)
                if h == 4:
                    dve.wait_ge(mod_done, 2)
                    dve.wait_ge(gates_b_ready, 16)
                    dve.wait_ge(mod_rows_ready, 1)
                    nc.vector.tensor_tensor(gates_b[:, :], bank[5][:, :], gates_b[:, :], ALU.add).then_inc(mod_rows_ready, 1)
            att_lo_part(CT - 1)

            def gn_centre(g):
                dve.wait_ge(gn_mean, g + 1)
                dve.wait_ge(tap, (g + 1) * len(TAPS) // 2)
                both = conv[:, 2 * g:2 * g + 2, :].rearrange("p a b -> p (a b)")
                nc.vector.tensor_tensor(both, both, bank[GN_BANK[g]][:, :], ALU.subtract).then_inc(gn_centred, 1)

            def gn_invert(g):
                dve.wait_ge(gn_std, g + 1)
                nc.vector.reciprocal(gn_rstd[:, g, :], gn_stat[:, g, :]).then_inc(gn_rs, 1)

            def gn_scale(g):
                dve.wait_ge(gn_bc, g + 1)
                dve.wait_ge(gn_sq, g + 1)
                for j in (2 * g, 2 * g + 1):
                    cut = slice((j % 2) * SEQ, (j % 2) * SEQ + SEQ)
                    nc.vector.scalar_tensor_tensor(conv[:, j, :], conv[:, j, :], col("gn_g", j), bank[GN_BANK[g]][:, cut],
                                                   ALU.mult, ALU.mult).then_inc(gn_scaled, 1)

            def mix_low(g):
                for j in (2 * g, 2 * g + 1):
                    dve.wait_ge(mix_hi, j + 1)
                    nc.vector.tensor_tensor(act_lo[:, CT + j, :], xmod[:, CT + j, :], act_hi[:, CT + j, :].bitcast(f32),
                                            ALU.subtract).then_inc(mix_lo, 1)

            mod_columns(1, "norm2_g", "sh2_b", "sc2_b")
            gn_centre(0)
            taps(12)
            gn_invert(0)
            taps(len(TAPS))
            split_lo(SP_AT["out", 3])
            gn_scale(0)
            gn_centre(1)
            mix_low(0)
            gn_invert(1)
            split_lo(SP_AT["up", 0])
            gn_scale(1)
            mix_low(1)
            split_lo(SP_AT["up", 1])
            dve.wait_ge(xr_ready, 16)
            for t in range(ST):
                for n in range(2):
                    i = 2 * t + n
                    cut = slice(n * 512, (n + 1) * 512)
                    dve.wait_ge(mixed, t + 1)
                    dve.wait_ge(gate_ready, n + 1)
                    if i >= 2:
                        dve.wait_ge(x2_ready, i - 1)
                    nc.vector.tensor_tensor(tmp[:, i % 2, :], bank[i][:, :], gate[:, 0, cut], ALU.mult).then_inc(x2_part, 1)
                    dve.wait_ge(x2_part, i + 1)
                    nc.vector.tensor_tensor(xr[:, t, cut], xr[:, t, cut], tmp[:, i % 2, :], ALU.add).then_inc(x2_ready, 1)
            dve.wait_ge(x2_std, 1)
            nc.vector.reciprocal(rinv2[:, :], rms2[:, :]).then_inc(x2_rs, 1)
            dve.wait_ge(x2_rs, 1)
            dve.wait_ge(x2_ready, 2 * ST)
            for t in range(ST):
                nc.vector.tensor_scalar(xmod[:, 4 * t:4 * t + 4, :].rearrange("p a b -> p (a b)"), xr[:, t, :],
                                        rinv2[:, t:t + 1], None, ALU.mult).then_inc(x2_normed, 1)
            for k in range(KT):
                dve.wait_ge(x2_turned, k - k % 2 + 2)
                nc.vector.tensor_scalar(xt[:, k, :], bank[4 + k // 2][:, (k % 2) * SEQ:(k % 2) * SEQ + SEQ],
                                        scale[:, 1, k:k + 1], shift[:, 1, k:k + 1], ALU.mult, ALU.add).then_inc(xn2_full, 1)
            for k in range(KT):
                dve.wait_ge(xn2_hi, k + 1)
                nc.vector.tensor_tensor(act_lo[:, k, :], xt[:, k, :], act_hi[:, k, :].bitcast(f32),
                                        ALU.subtract).then_inc(xn2_lo, 1)

            def after_up(t):
                for g in range(2):
                    dve.wait_ge(tap2, 2 * t + g + 1)
                    nc.vector.scalar_tensor_tensor(ug[:, t % 2, g, 1:], bank[4 + 2 * (t % 2) + g][:, 0:SEQ - 1],
                                                   col("ffn_w", (g * FT + t) * FFN_TAPS + 1), ug[:, t % 2, g, 1:],
                                                   ALU.mult, ALU.add).then_inc(tap1, 1)
                for g in range(2):
                    dve.wait_ge(tap1, 2 * t + g + 1)
                    nc.vector.scalar_tensor_tensor(ug[:, t % 2, g, 2:], bank[4 + 2 * (t % 2) + g][:, 0:SEQ - 2],
                                                   col("ffn_w", (g * FT + t) * FFN_TAPS), ug[:, t % 2, g, 2:],
                                                   ALU.mult, ALU.add).then_inc(tap0, 1)
                dve.wait_ge(gated, t + 1)
                if t >= 2:
                    dve.wait_ge(hid_lo_ready, t - 1)
                nc.vector.tensor_tensor(hid[:, t % 2, :], ug[:, t % 2, 0, :], silu_g[:, t % 2, :],
                                        ALU.mult).then_inc(hidden, 1)

            def hid_low(t):
                dve.wait_ge(hid_hi_ready, t + 1)
                if t >= 4:
                    dve.wait_ge(w_used, SP_AT["down", t // 2 - 2] + 1)
                nc.vector.tensor_tensor(hid_lo[:, t % 4, :], hid[:, t % 2, :], hid_hi[:, t % 4, :].bitcast(f32),
                                        ALU.subtract).then_inc(hid_lo_ready, 1)

            m0 = SP_AT["up", 0]
            for m in range(m0, len(SPLIT)):
                split_lo(m + 2)
                if m > m0 and SPLIT[m - 1][0] == "up":
                    after_up(SPLIT[m - 1][1])
                    hid_low(SPLIT[m - 1][1])
            dve.wait_ge(gate_ready, 4)
            for t in range(ST):
                for n in range(2):
                    dve.wait_ge(down_done, t + 1)
                    i = 2 * t + n
                    cut = slice(n * 512, (n + 1) * 512)
                    if i >= 2:
                        dve.wait_ge(out_ready, i - 1)
                    nc.vector.tensor_tensor(tmp[:, i % 2, :], bank[i][:, :], gate[:, 1, cut], ALU.mult).then_inc(out_part, 1)
                    dve.wait_ge(out_part, i + 1)
                    nc.vector.tensor_tensor(xmod[:, 4 * t + 2 * n:4 * t + 2 * n + 2, :].rearrange("p a b -> p (a b)"),
                                            xr[:, t, cut], tmp[:, i % 2, :], ALU.add).then_inc(out_ready, 1)

        @block.tensor
        def _(pe):
            def product(o, stat, mov, first, last):
                (sh, sl), (mh, ml) = stat, mov
                nc.tensor.matmul(o, sh, mh, start=first, stop=False)
                nc.tensor.matmul(o, sh, ml, start=False, stop=False)
                return nc.tensor.matmul(o, sl, mh, start=False, stop=last)

            def weights(m, a, n):
                hi, lo = parts(m)
                return hi[:, a:a + n], lo[:, a:a + n]

            def acts(k, a, n):
                return act_hi[:, k, a:a + n], act_lo[:, k, a:a + n]

            def ready(m):
                pe.wait_ge(lo_done, m + 1)
                pe.wait_ge(hi_done, m + 1)

            def ada(n, to):
                arrived(pe, "ada", n)
                k = n % KT
                for q in range(4):
                    last = nc.tensor.matmul(bank[to][32 * q:32 * q + 32, :], silu_c[:, k:k + 1].to_broadcast([P, 32]),
                                            slot("ada", n)[:, 512 * q:512 * q + 512], start=(k == 0), stop=(k == KT - 1))
                last.then_inc(ada_used, 1)

            def turn_mod_rows(to):
                for j in range(4):
                    last = nc.tensor.transpose(bank[to][:, j * P:(j + 1) * P], mod_rows[:, j * P:(j + 1) * P], ident[:, :])
                last.then_inc(mod_cols_ready, 1)

            pe.wait_ge(consts_ready, 1)
            pe.wait_ge(xsq_ready, 1)
            for k in range(KT):
                last = nc.tensor.matmul(bank[7][:, 0:SEQ], ones[:, :], xmod[:, k, :], start=(k == 0), stop=(k == KT - 1))
            last.then_inc(ssq_ready, 1)
            pe.wait_ge(silu_c_ready, 1)
            for k in range(KT):
                ada(k, 0)
            pe.wait_ge(ada_used, KT)
            nc.tensor.transpose(bank[2][:, 0:P], ident[:, :], ident[:, :]).then_inc(mod_done, 1)
            pe.wait_ge(mod_rows_ready, 1)
            turn_mod_rows(1)

            def pair(m, to):
                for c in range(2):
                    for k in range(KT):
                        if m == 0 and c == 0:
                            pe.wait_ge(xn_hi, k + 1)
                            pe.wait_ge(xn_lo, k + 1)
                        last = product(bank[to][:, c * SEQ:(c + 1) * SEQ], weights(m, k * 2 * P + c * P, P),
                                       acts(k, 0, SEQ), k == 0, k == KT - 1)
                last.then_inc(w_used, 1)

            pe.wait_ge(mod_cols_read, 2)
            for j in range(CT):
                m = SP_AT["conv", j]
                ready(m)
                if j >= 2:
                    pe.wait_ge(glu_ready, j - 1)
                pair(m, j % 2)

            def qk_squares(j):
                pe.wait_ge(qk_sq_ready, j + 1)
                for part in range(2):
                    last = nc.tensor.matmul(bank[6][0:16, 0:SEQ], to_group[:, 4 * part + j, :],
                                            qk_sq[:, j % 2, part * SEQ:(part + 1) * SEQ],
                                            start=(j == 0 and part == 0), stop=(j == CT - 1 and part == 1))
                last.then_inc(qk_ssq, 1)

            for j in range(CT):
                m = SP_AT["qk", j]
                ready(m)
                if j < 2:
                    pe.wait_ge(glu_ready, CT - 1 + j)
                else:
                    pe.wait_ge(qk_sq_ready, j - 1)
                pair(m, j % 2)
                if j >= 1:
                    qk_squares(j - 1)
            for i in range(2):
                m = SP_AT["v", i]
                ready(m)
                for t in range(ST):
                    for k in range(KT // 2):
                        kk = i * KT // 2 + k
                        last = product(bank[4 + t][:, :], acts(kk, t * P, P), weights(m, k * 512, 512),
                                       kk == 0, kk == KT - 1)
                last.then_inc(w_used, 1)
                if i == 0:
                    qk_squares(CT - 1)
            pe.wait_ge(qk_rs, 1)
            for j in range(CT):
                if j >= 2:
                    pe.wait_ge(qk_normed, 2 * (j - 1))
                else:
                    pe.wait_ge(qk_sq_ready, CT)
                for part in range(2):
                    last = nc.tensor.matmul(bank[j % 2][:, part * SEQ:(part + 1) * SEQ], from_group[:, 4 * part + j, :],
                                            qk_rstd[:, :], start=True, stop=True)
                last.then_inc(qk_bc, 1)

            def head_scores(h):
                j, r = h // 2, slice(64 * (h % 2), 64 * (h % 2) + 64)
                pe.wait_ge(qk_normed, max(2 * (j + 1), 2 * CT if h < 2 else 0))
                if h >= 3:
                    pe.wait_ge(biased, 2 * (h - 2))
                for t, (a, b, _) in enumerate(ROWS):
                    last = nc.tensor.matmul(bank[h % 3][:, a:b], qk[r, j, t * P:(t + 1) * P], qk[r, j, SEQ:SEQ + b - a],
                                            start=True, stop=True)
                last.then_inc(scores, 1)

            def head_turn(h):
                pe.wait_ge(normed, h + 1)
                if h >= 2:
                    pe.wait_ge(turned_copied, h - 1)
                for t in range(3):
                    last = nc.tensor.transpose(bank[3 + h % 2][:, t * P:(t + 1) * P], prob[:, h % 3, t * P:(t + 1) * P],
                                               ident[:, :])
                last.then_inc(turned, 1)

            def head_values(h):
                pe.wait_ge(turned_copied, h + 1)
                r = slice(64 * (h % 2), 64 * (h % 2) + 64)
                if h % 2 == 0 and h >= 2:
                    pe.wait_ge(att_lo, h // 2)
                nc.tensor.matmul(bank[6][r, 0:SEQ], v[:, 0, h * 64:(h + 1) * 64], prob_t[:, h % 2, 0:SEQ],
                                 start=True, stop=False)
                nc.tensor.matmul(bank[6][r, P:SEQ], v[:, 1, h * 64:(h + 1) * 64], prob_t[:, h % 2, SEQ:384],
                                 start=False, stop=True).then_inc(attended, 1)

            pe.wait_ge(v_ready, ST)
            head_scores(0)
            for h in range(HEADS):
                if h + 1 < HEADS:
                    head_scores(h + 1)
                if h == 4:
                    pe.wait_ge(mod_rows_ready, 2)
                ada(KT + 2 * h, 5)
                ada(KT + 2 * h + 1, 5)
                if h == 3 or h == HEADS - 1:
                    pe.wait_ge(ada_used, KT + 2 * h + 2)
                    nc.tensor.transpose(bank[7][:, 0:P], ident[:, :], ident[:, :]).then_inc(mod_done, 1)
                head_turn(h)
                if h >= 1:
                    head_values(h - 1)
            head_values(HEADS - 1)

            def out_tile(k, tiles=range(ST)):
                m = SP_AT["out", k // 2]
                for t in tiles:
                    for n in range(2):
                        last = product(bank[2 * t + n][:, :], acts(k, t * P, P),
                                       weights(m, (k % 2) * D_MODEL + n * 512, 512), k == 0, k == KT - 1)
                return last

            def gn_means(g):
                pe.wait_ge(tap, (g + 1) * len(TAPS) // 2)
                for c in range(2):
                    last = nc.tensor.matmul(bank[GN_BANK[g]][:, c * SEQ:(c + 1) * SEQ], half_mean[:, :],
                                            conv[:, 2 * g + c, :], start=True, stop=True)
                last.then_inc(gn_mean, 1)

            def gn_squares(g):
                pe.wait_ge(gn_sq, g + 1)
                if g == 1:
                    pe.wait_ge(gn_std, 1)
                for c in range(2):
                    last = nc.tensor.matmul(bank[7][0:4, 0:SEQ], to_group[:, c, 0:4], xmod[:, 2 * g + c, :],
                                            start=(c == 0), stop=(c == 1))
                last.then_inc(gn_ssq, 1)

            def gn_spread(g):
                pe.wait_ge(gn_rs, g + 1)
                for c in range(2):
                    last = nc.tensor.matmul(bank[GN_BANK[g]][:, c * SEQ:(c + 1) * SEQ], from_group[0:4, c, :],
                                            gn_rstd[:, g, :], start=True, stop=True)
                last.then_inc(gn_bc, 1)

            def spread_gate(n):
                pe.wait_ge(gn_scaled, 2)
                if n >= 2:
                    pe.wait_ge(gate_ready, n - 1)
                nc.tensor.matmul(bank[4 + n % 2][:, :], ones[32 * n:32 * n + 1, :], gates_b[32 * n:32 * n + 1, :],
                                 start=True, stop=True, tile_position=(32 * n, 0)).then_inc(gate_bc, 1)

            pe.wait_ge(turned_copied, HEADS)
            pe.wait_ge(biased, 2 * HEADS)
            pe.wait_ge(mod_rows_ready, 3)
            turn_mod_rows(5)
            gn_means(0)
            pe.wait_ge(att_lo, CT)
            ready(SP_AT["out", 0])
            out_tile(0)
            out_tile(1).then_inc(w_used, 1)
            gn_squares(0)
            ready(SP_AT["out", 1])
            out_tile(2)
            gn_spread(0)
            gn_means(1)
            out_tile(3).then_inc(w_used, 1)
            ready(SP_AT["out", 2])
            gn_squares(1)
            pe.wait_ge(mix_lo, 1)
            out_tile(4)
            pe.wait_ge(mod_cols_read, 4)
            spread_gate(0)
            spread_gate(1)
            gn_spread(1)
            pe.wait_ge(mix_lo, 2)
            out_tile(5).then_inc(w_used, 1)
            spread_gate(2)
            spread_gate(3)
            ready(SP_AT["out", 3])
            pe.wait_ge(mix_lo, CT)
            for t in range(ST):
                out_tile(6, [t])
                last = out_tile(7, [t])
                last.then_inc(mixed, 1)
            nc.tensor.transpose(bank[7][:, 0:P], ident[:, :], ident[:, :]).then_inc(w_used, 1)
            pe.wait_ge(gate_ready, 4)
            pe.wait_ge(x2_normed, ST)
            for k in range(KT):
                for t in range(ST):
                    last = nc.tensor.transpose(bank[4 + k // 2][:, (k % 2) * SEQ + t * P:(k % 2) * SEQ + (t + 1) * P],
                                               xmod[:, 4 * t + k // 2, (k % 2) * P:(k % 2) * P + P], ident[:, :])
                last.then_inc(x2_turned, 1)

            def up(t):
                m = SP_AT["up", t]
                ready(m)
                if t >= 2:
                    pe.wait_ge(tap0, 2 * (t - 1))
                for g in range(2):
                    for k in range(KT):
                        if t == 0 and g == 0:
                            pe.wait_ge(xn2_lo, KT)
                        last = product(bank[4 + 2 * (t % 2) + g][:, 0:SEQ], weights(m, k * 2 * P + g * P, P),
                                       acts(k, 0, SEQ), k == 0, k == KT - 1)
                last.then_inc(w_used, 1)

            def down(i):
                m = SP_AT["down", i]
                ready(m)
                pe.wait_ge(hid_lo_ready, 2 * i + 2)
                pe.wait_ge(hid_hi_ready, 2 * i + 2)
                order = [(f, t) for f in range(2) for t in range(ST)] if i < FT // 2 - 1 else \
                        [(f, t) for t in range(ST) for f in range(2)]
                for f, t in order:
                    place = (2 * i + f) % 4
                    h = (hid_hi[:, place, t * P:(t + 1) * P], hid_lo[:, place, t * P:(t + 1) * P])
                    for n in range(2):
                        last = product(bank[2 * t + n][:, :], h, weights(m, f * D_MODEL + n * 512, 512),
                                       i == 0 and f == 0, i == FT // 2 - 1 and f == 1)
                    if i == FT // 2 - 1 and f == 1:
                        last.then_inc(down_done, 1)
                if i < FT // 2 - 1:
                    last.then_inc(w_used, 1)

            pe.wait_ge(x2_ready, 2 * ST)
            for kind, i in UP_DOWN:
                (up if kind == "up" else down)(i)


def _layout(x, c, rel_bias, ada_w, ada_b, norm1_g, w_in, q_norm_g, k_norm_g, conv_dw_w, conv_dw_b, conv_norm_g,
            conv_norm_b, w_out, norm2_g, w_up, ffn_dw_w, ffn_dw_b, w_down):
    a = {k: np.asarray(v) for k, v in locals().items()}

    def by_tile(v):
        return v.reshape(-1, P).T

    def pairs(w, first, second, n):
        w = w.reshape(KT, P, -1, P)
        return [np.stack([w[:, :, first + j], w[:, :, second + j]], 2).transpose(1, 0, 2, 3).reshape(P, SLOT)
                for j in range(n)]

    ada = a["ada_w"][0].reshape(KT, P, 12, 512)
    w_in = a["w_in"][0]
    slots = {}
    for g, chunks in enumerate(ADA_GROUPS):
        for k in range(KT):
            slots["ada", g * KT + k] = ada[k][:, list(chunks)].reshape(P, SLOT)
    for j, s in enumerate(pairs(w_in, 16, 12, CT)):
        slots["conv", j] = s
    for j, s in enumerate(pairs(w_in, 0, 4, CT)):
        slots["qk", j] = s
    wv = w_in[:, 1024:1536].reshape(2, KT // 2, P, 512)
    for i in range(2):
        slots["v", i] = wv[i].transpose(1, 0, 2).reshape(P, SLOT)
    wo = a["w_out"][0].reshape(4, 2, P, D_MODEL)
    for j in range(4):
        slots["out", j] = wo[j].transpose(1, 0, 2).reshape(P, SLOT)
    for t, s in enumerate(pairs(a["w_up"][0], 0, FT, FT)):
        slots["up", t] = s
    wd = a["w_down"][0].reshape(FT // 2, 2, P, D_MODEL)
    for i in range(FT // 2):
        slots["down", i] = wd[i].transpose(1, 0, 2).reshape(P, SLOT)
    stream = np.stack([slots[s] for s in STREAM])

    b = a["ada_b"][0].reshape(6, D_MODEL)
    parts = {
        "c": by_tile(a["c"][0]), "norm1_g": by_tile(a["norm1_g"][0]), "norm2_g": by_tile(a["norm2_g"][0]),
        "sh1_b": by_tile(b[0]), "sc1_b": by_tile(b[1]), "sh2_b": by_tile(b[3]), "sc2_b": by_tile(b[4]),
        "conv_w": a["conv_dw_w"][0].reshape(CONV_TAPS, CT, P).transpose(2, 1, 0).reshape(P, -1),
        "conv_b": by_tile(a["conv_dw_b"][0]), "gn_g": by_tile(a["conv_norm_g"][0]), "gn_b": by_tile(a["conv_norm_b"][0]),
        "ffn_w": a["ffn_dw_w"][0].reshape(FFN_TAPS, 2 * FT, P).transpose(2, 1, 0).reshape(P, -1),
        "ffn_b": by_tile(a["ffn_dw_b"][0]),
        "q_g": np.tile(a["q_norm_g"][0], 2)[:, None], "k_g": np.tile(a["k_norm_g"][0], 2)[:, None],
    }
    cols = np.concatenate([parts[k] for k in COLS], axis=1)
    x2 = a["x"][0]
    return {
        "stream": stream,
        "x_t": x2.T.reshape(KT, P, SEQ).transpose(1, 0, 2),
        "x_rows": x2.reshape(ST, P, D_MODEL).transpose(1, 0, 2),
        "cols": cols,
        "ada_b_gates": np.repeat(a["ada_b"][0].reshape(12, 512)[list(ADA_GROUPS[1])], 32, axis=0),
        "rel_bias": a["rel_bias"],
    }


def kernel(**inputs):
    import concourse.bacc as _bacc
    from concourse.bass_utils import run_bass_kernel_spmd as _run

    nc = _bacc.Bacc("TRN2", target_bir_lowering=False, num_devices=1)
    arrays, args = {}, []
    for name, a in _layout(**inputs).items():
        a = np.ascontiguousarray(a)
        arrays[f"in_{name}"] = a
        args.append(nc.dram_tensor(f"in_{name}", a.shape, mybir.dt.from_np(a.dtype), kind="ExternalInput").ap())
    out = nc.dram_tensor("out_0", (ST, P, D_MODEL), mybir.dt.float32, kind="ExternalOutput").ap()
    hymba_layer(nc, *args, out)
    r = _run(nc, [arrays], core_ids=[0])
    return r.results[0]["out_0"].reshape(1, SEQ, D_MODEL)
```

```python
import math
from contextlib import ExitStack

import numpy as np

import concourse.bass as bass
from concourse import mybir

D_MODEL, SEQ = 1024, 256
HEADS, HEAD_DIM = 8, 64
CONV_TAPS, FFN_TAPS = 31, 3
FFN_HIDDEN = 2816
N_BUCKETS, MAX_DISTANCE = 32, 1024
EPS, NEG = 1e-6, -1e30

P = 128
KT = D_MODEL // P
ST = SEQ // P
CT = D_MODEL // 2 // P
FT = FFN_HIDDEN // P
SLOT = 2048
HALF = SLOT // 2

ADA_GROUPS = [(0, 1, 2, 3), (4, 5, 10, 11), (6, 7, 8, 9)]
UP_DOWN = [("up", 0), ("up", 1)]
for _i in range(FT // 2):
    if _i + 1 < FT // 2:
        UP_DOWN += [("up", 2 * _i + 2), ("up", 2 * _i + 3)]
    UP_DOWN += [("down", _i)]
ADA_AFTER = {("conv", 1): 1, ("conv", 2): 1, ("conv", 3): 1, ("qk", 0): 1, ("qk", 1): 1, ("qk", 2): 1, ("qk", 3): 2}
ADA_AT_HEAD = (2, 2, 1)
STREAM = [("ada", k) for k in range(KT)] + [("conv", 0)]
_ada = KT
for _s in [("conv", j) for j in range(1, CT)] + [("qk", j) for j in range(CT)] + [("v", 0), ("v", 1)]:
    STREAM.append(_s)
    for _ in range(ADA_AFTER.get(_s, 0)):
        STREAM.append(("ada", _ada))
        _ada += 1
ADA_LATE = range(_ada, 3 * KT)
STREAM += [("ada", n) for n in ADA_LATE] + [("out", j) for j in range(4)] + UP_DOWN
OUT_TILES = [0, 1, 4, 5, 6, 7, 2, 3]
SPLIT = [x for x in STREAM if x[0] != "ada"]
AT = {x: n for n, x in enumerate(STREAM)}
SP_AT = {x: m for m, x in enumerate(SPLIT)}
RAW, PARTS = 6, 3

COLS = {}
_at = 0
for _name, _n in [("c", KT), ("norm1_g", KT), ("norm2_g", KT), ("sh1_b", KT), ("sc1_b", KT), ("sh2_b", KT),
                  ("sc2_b", KT), ("conv_w", CT * CONV_TAPS), ("conv_b", CT), ("gn_g", CT), ("gn_b", CT),
                  ("ffn_w", 2 * FT * FFN_TAPS), ("ffn_b", 2 * FT), ("q_g", 1), ("k_g", 1)]:
    COLS[_name] = (_at, _n)
    _at += _n
N_COLS = _at

LEAD = 20
TAPS = [(1, i) for i in range(LEAD)]
TAPS += [(t, i - LEAD * (t == 3)) for i in range(LEAD, CONV_TAPS) for t in (1, 3)]
TAPS += [(3, i) for i in range(CONV_TAPS - LEAD, CONV_TAPS)]
PAIR_TAPS = (TAPS.index((1, CONV_TAPS - 1)) + 1, len(TAPS))
MULTS = [(t, i) for t in (0, 2) for i in range(CONV_TAPS)]
MULTS_PER_STEP = 7


def bucket_ranges():
    d = np.arange(SEQ)
    exact = N_BUCKETS // 2
    nf = np.maximum(d, 1).astype(np.float32)
    large = exact + (np.log(nf / np.float32(exact)) / np.float32(math.log(MAX_DISTANCE / exact))
                     * np.float32(N_BUCKETS - exact)).astype(np.int32)
    b = np.where(d < exact, d, np.minimum(large, N_BUCKETS - 1))
    return [(int(v), int(d[b == v][0]), int(d[b == v][-1])) for v in np.unique(b)]


def hymba_layer(nc, stream, x_t, x_rows, cols_in, ada_b_gates, rel_bias, out):
    f32, f32r = mybir.dt.float32, mybir.dt.float32r
    ALU, ACT = mybir.AluOpType, mybir.ActivationFunctionType

    toeplitz_rows = nc.dram_tensor("toeplitz_rows", [HEADS, 384], f32, kind="Internal").ap()

    ctx = ExitStack()
    with ctx:
        def sb(name, shape, dt=f32):
            return ctx.enter_context(nc.sbuf_tensor(name, shape, dt))

        def sem(name):
            return ctx.enter_context(nc.semaphore(name))

        bank = [ctx.enter_context(nc.psum_tensor(f"bank{i}", [P, 512], f32)) for i in range(8)]

        raw = sb("raw", [P, RAW, SLOT])
        w_hi = sb("w_hi", [P, PARTS, SLOT], f32r)
        w_lo = sb("w_lo", [P, PARTS, SLOT], f32r)
        xt = sb("xt", [P, KT, SEQ])
        xmod = sb("xmod", [P, KT, SEQ])
        act_hi = sb("act_hi", [P, KT, SEQ], f32r)
        act_lo = sb("act_lo", [P, KT, SEQ], f32r)
        xr = sb("xr", [P, ST, D_MODEL])
        gate = sb("gate", [P, 2, D_MODEL])
        cols = sb("cols", [P, N_COLS])
        silu_c = sb("silu_c", [P, KT])
        gates_b = sb("gates_b", [P, 512])
        mod_rows = sb("mod_rows", [P, 512])
        scale = sb("scale", [P, 2, KT])
        shift = sb("shift", [P, 2, KT])
        rms = sb("rms", [P, SEQ])
        rinv = sb("rinv", [P, SEQ])
        ident = sb("ident", [P, P])
        ones = sb("ones", [P, P])
        half_mean = sb("half_mean", [P, P])
        to_group = sb("to_group", [P, 8, 16])
        from_group = sb("from_group", [16, 8, P])
        table = sb("table", [HEADS, N_BUCKETS])
        bias_rows = sb("bias_rows", [HEADS, 384])
        bias = sb("bias", [P, HEADS, SEQ])
        glu_gate = sb("glu_gate", [P, 2, SEQ])
        glu = sb("glu", [P, CT, SEQ + CONV_TAPS - 1])
        conv = sb("conv", [P, CT, SEQ])
        gn_stat = sb("gn_stat", [P, ST * 8])
        gn_inv = sb("gn_inv", [P, ST * 8])
        gn_rstd = sb("gn_rstd", [8, SEQ])
        qk = sb("qk", [P, CT, 2 * SEQ])
        qk_sq = gate[:, 0, :].rearrange("p (a b) -> p a b", a=2)
        qk_stat = sb("qk_stat", [P, ST * 16])
        qk_inv = sb("qk_inv", [P, ST * 16])
        qk_rstd = sb("qk_rstd", [16, SEQ])
        q_gain = sb("q_gain", [P, 1])
        v = gate[:, 1, :].rearrange("p (t n) -> p t n", t=ST)
        prob = sb("prob", [P, 3, 384])
        prob_t = sb("prob_t", [P, 2, 384])
        peak = sb("peak", [P, 2 * HEADS])
        npeak = sb("npeak", [P, 2 * HEADS])
        total = sb("total", [P, 2 * HEADS])
        rtotal = sb("rtotal", [P, 2 * HEADS])
        ssq2 = sb("ssq2", [P, 2 * ST])
        half2 = sb("half2", [P, ST])
        diag = sb("diag", [P, ST, P])
        rms2 = sb("rms2", [P, ST])
        rinv2 = sb("rinv2", [P, ST])
        tmp = qk
        ug = bias[:, 0:4, :].rearrange("p (t g) s -> p t g s", t=2)
        silu_g = bias[:, 4:6, :]
        hid = bias[:, 6:8, :]
        hid_hi = sb("hid_hi", [P, 4, SEQ], f32r)
        hid_lo = sb("hid_lo", [P, 4, SEQ], f32r)
        eps = sb("eps", [P, 1])

        raw_ready = [sem(f"raw_ready{i}") for i in range(RAW)]
        cols_ready, xt_ready, xr_ready = sem("cols_ready"), sem("xt_ready"), sem("xr_ready")
        gates_b_ready, table_ready = sem("gates_b_ready"), sem("table_ready")
        rows_stored, bias_ready = sem("rows_stored"), sem("bias_ready")
        half_ready, half_hi, half_lo = sem("half_ready"), sem("half_hi"), sem("half_lo")
        pool_step, consts_ready = sem("pool_step"), sem("consts_ready")
        ada_used, w_used = sem("ada_used"), sem("w_used")
        hi_done, lo_done = sem("hi_done"), sem("lo_done")
        silu_c_ready, xsq_ready, ssq_ready, rms_ready = (sem(s) for s in ("silu_c_ready", "xsq_ready", "ssq_ready", "rms_ready"))
        mod_done, mod_rows_ready, mod_cols_ready = sem("mod_done"), sem("mod_rows_ready"), sem("mod_cols_ready")
        mod_cols_read = sem("mod_cols_read")
        gate_bc, gate_ready, gate2_ready = sem("gate_bc"), sem("gate_ready"), sem("gate2_ready")
        xn_full, xn_hi, xn_lo, xn_lo_pool = (sem(s) for s in ("xn_full", "xn_hi", "xn_lo", "xn_lo_pool"))
        sig_ready, glu_ready = sem("sig_ready"), sem("glu_ready")
        tap, tap_mult, pool_tap = sem("tap"), sem("tap_mult"), sem("pool_tap")
        qk_raw, qk_sq_ready, qk_ssq, qk_std, qk_inverted, qk_turned, qk_rs, qk_bc, qk_normed = (
            sem(s) for s in ("qk_raw", "qk_sq_ready", "qk_ssq", "qk_std", "qk_inverted", "qk_turned", "qk_rs", "qk_bc", "qk_normed"))
        v_ready, rinv_ready, xhat_ready, mixed = sem("v_ready"), sem("rinv_ready"), sem("xhat_ready"), sem("mixed")
        scores, biased, peaked, exped, inverted, normed, turned, turned_copied, attended, att_hi, att_lo = (
            sem(s) for s in ("scores", "biased", "peaked", "exped", "inverted", "normed", "turned", "turned_copied",
                             "attended", "att_hi", "att_lo"))
        gn_mean, gn_centred, gn_sq, gn_ssq, gn_std, gn_inverted, gn_turned, gn_rs, gn_bc, gn_scaled, gn_silu, mix_hi, mix_lo = (
            sem(s) for s in ("gn_mean", "gn_centred", "gn_sq", "gn_ssq", "gn_std", "gn_inverted", "gn_turned", "gn_rs", "gn_bc", "gn_scaled",
                             "gn_silu", "mix_hi", "mix_lo"))
        x2_part, x2_left, x2_right, x2_sq, x2_half, x2_std, x2_rs, x2_diag, x2_turned, xn2_full, xn2_hi, xn2_lo, xn2_lo_pool = (
            sem(s) for s in ("x2_part", "x2_left", "x2_right", "x2_sq", "x2_half", "x2_std", "x2_rs", "x2_diag", "x2_turned",
                             "xn2_full", "xn2_hi", "xn2_lo", "xn2_lo_pool"))
        tap2, tap1, tap0, gated, hidden, hid_hi_ready, hid_lo_ready, down_done = (
            sem(s) for s in ("tap2", "tap1", "tap0", "gated", "hidden", "hid_hi_ready", "hid_lo_ready", "down_done"))
        out_part, out_ready, stored = sem("out_part"), sem("out_ready"), sem("stored")

        def col(name, i=0):
            a, _ = COLS[name]
            return cols[:, a + i:a + i + 1]

        def cols_of(name):
            a, n = COLS[name]
            return cols[:, a:a + n]

        def slot(kind, i):
            return raw[:, AT[kind, i] % RAW, :]

        def arrived(eng, kind, i):
            n = AT[kind, i]
            eng.wait_ge(raw_ready[n % RAW], 16 * (n // RAW + 1))

        def parts(m):
            return w_hi[:, m % PARTS, :], w_lo[:, m % PARTS, :]

        def tap_prod(n):
            return xmod[:, n % KT, :]

        POOL_LOWS = 3

        ROWS = [(0, P, P), (P, 384, 0)]
        GN_BANK = (6, 5)
        OUT_BANK = 4

        HIGH_AT_HEAD = {0: SP_AT["out", 0], 2: SP_AT["out", 1], 4: SP_AT["out", 2], 5: SP_AT["out", 3], 6: SP_AT["up", 0]}
        LOW_AT_HEAD = {1: SP_AT["out", 0], 4: SP_AT["out", 1], 5: SP_AT["out", 2], 6: SP_AT["out", 3], 7: SP_AT["up", 0]}

        block = ctx.enter_context(nc.Block())

        @block.sync
        def _(sp):
            sp.dma_start(cols[:, :], cols_in).then_inc(cols_ready, 16)
            for n, (kind, i) in enumerate(STREAM):
                if n >= RAW:
                    k0, i0 = STREAM[n - RAW]
                    if k0 == "ada":
                        sp.wait_ge(ada_used, i0 + 1)
                    else:
                        sp.wait_ge(lo_done, SP_AT[k0, i0] + 1)
                if (kind, i) == ("conv", 0):
                    sp.dma_start(raw[:, n % RAW, 0:HALF], stream[n, :, 0:HALF]).then_inc(half_ready, 16)
                    sp.dma_start(raw[:, n % RAW, HALF:], stream[n, :, HALF:]).then_inc(raw_ready[n % RAW], 16)
                else:
                    sp.dma_start(raw[:, n % RAW, :], stream[n]).then_inc(raw_ready[n % RAW], 16)
                if n == 0:
                    sp.dma_start(xt[:, :, :], x_t).then_inc(xt_ready, 16)
                if (kind, i) == ("v", 1):
                    sp.wait_ge(rows_stored, 16)
                    sp.dma_start(bias[:, :, :], bass.AP(toeplitz_rows.tensor, 0, [[1, P], [384, HEADS], [1, SEQ]])
                                 ).then_inc(bias_ready, 16)
                if (kind, i) == ("qk", 3):
                    sp.dma_start(gates_b[:, :], ada_b_gates).then_inc(gates_b_ready, 16)
                if (kind, i) == ("up", 0):
                    sp.dma_start(xr[:, :, :], x_rows).then_inc(xr_ready, 16)
            for t in range(ST):
                for n in range(2):
                    sp.wait_ge(out_ready, 2 * t + n + 1)
                    sp.dma_start(out[t, :, n * 512:(n + 1) * 512], xmod[:, 4 * t + 2 * n:4 * t + 2 * n + 2, :].rearrange("p a b -> p (a b)")).then_inc(stored, 16)
            sp.wait_ge(stored, 16 * 2 * ST)

        @block.gpsimd
        def _(pool):
            step = [0]

            def chained(ins):
                step[0] += 1
                ins.then_inc(pool_step, 1)
                pool.wait_ge(pool_step, step[0])

            pool.dma_start(table[:, :], rel_bias).then_inc(table_ready, 16)
            chained(nc.gpsimd.memset(eps[:, :], EPS))
            chained(nc.gpsimd.memset(ones[:, :], 1.0))
            chained(nc.gpsimd.memset(half_mean[:, :], 0.0))
            chained(nc.gpsimd.memset(glu[:, :, 0:CONV_TAPS - 1], 0.0))
            chained(nc.gpsimd.memset(from_group[:, :, :], 0.0))
            chained(nc.gpsimd.memset(to_group[:, :, :], 0.0))
            chained(nc.gpsimd.memset(ident[:, :], 0.0))
            flat = to_group[:, :, :].rearrange("p j m -> p (j m)")
            for half in range(2):
                rows = slice(64 * half, 64 * half + 64)
                chained(nc.gpsimd.memset(flat[rows, half:128:18], 1.0))
                chained(nc.gpsimd.memset(half_mean[rows, rows], 1.0 / 64))
            chained(nc.gpsimd.affine_select(out=ident[:, :], in_=ident[:, :], compare_op=ALU.not_equal, fill=1.0,
                                            base=0, pattern=[[-1, P]], channel_multiplier=1))
            wide = from_group[:, :, :].rearrange("p j (a c) -> p j a c", a=2)
            nc.gpsimd.affine_select(out=wide, in_=wide, compare_op=ALU.not_equal, fill=1.0, base=0,
                                    pattern=[[-2, 8], [-1, 2], [0, 64]], channel_multiplier=1).then_inc(consts_ready, 1)
            pool.wait_ge(table_ready, 16)
            chained(nc.gpsimd.memset(bias_rows[:, 0:P - 1], NEG))
            chained(nc.gpsimd.memset(bias_rows[:, 383:384], NEG))
            for b, lo, hi in bucket_ranges():
                n = hi - lo + 1
                chained(nc.gpsimd.tensor_copy(bias_rows[:, P - 1 + lo:P + hi],
                                              table[:, b:b + 1].to_broadcast([HEADS, n])))
            pool.dma_start(toeplitz_rows, bias_rows[:, :]).then_inc(rows_stored, 16)
            for k in range(POOL_LOWS):
                pool.wait_ge(xn_full, k + 1)
                pool.wait_ge(xn_hi, k + 1)
                nc.gpsimd.tensor_tensor(act_lo[:, k, :], xmod[:, k, :], act_hi[:, k, :].bitcast(f32),
                                        ALU.subtract).then_inc(xn_lo_pool, 1)
            added = 0
            for n, (j, i) in enumerate(MULTS):
                if i == 0:
                    continue
                pool.wait_ge(tap_mult, n + 1)
                if i >= 2:
                    pool.wait_ge(pool_tap, added)
                nc.gpsimd.tensor_tensor(conv[:, j, :], conv[:, j, :], tap_prod(n), ALU.add).then_inc(pool_tap, 1)
                added += 1
            for g in range(2):
                pool.wait_ge(gn_centred, g + 1)
                if g == 1:
                    pool.wait_ge(pool_tap, len(MULTS) - 2)
                nc.gpsimd.tensor_tensor(xmod[:, 2 * g:2 * g + 2, :], conv[:, 2 * g:2 * g + 2, :],
                                        conv[:, 2 * g:2 * g + 2, :], ALU.mult).then_inc(gn_sq, 1)
            pool.wait_ge(xr_ready, 16)
            for t in range(ST):
                pool.wait_ge(x2_part, 2 * t + 1)
                nc.gpsimd.tensor_tensor(xr[:, t, 0:512], xr[:, t, 0:512], tmp[:, 2 * t, :], ALU.add).then_inc(x2_left, 1)
            for k in range(1, KT, 2):
                pool.wait_ge(xn2_hi, k + 1)
                nc.gpsimd.tensor_tensor(act_lo[:, k, :], xt[:, k, :], act_hi[:, k, :].bitcast(f32),
                                        ALU.subtract).then_inc(xn2_lo_pool, 1)

        @block.scalar
        def _(act):
            def split_hi(m):
                if m >= len(SPLIT):
                    return
                arrived(act, *SPLIT[m])
                if m >= PARTS:
                    act.wait_ge(w_used, m - PARTS + 1)
                nc.scalar.activation(w_hi[:, m % PARTS, :], slot(*SPLIT[m]), ACT.Copy).then_inc(hi_done, 1)

            act.wait_ge(cols_ready, 16)
            nc.scalar.activation(silu_c[:, :], cols_of("c"), ACT.Silu).then_inc(silu_c_ready, 1)
            act.wait_ge(xt_ready, 16)
            nc.scalar.activation(xmod[:, :, :], xt[:, :, :], ACT.Square).then_inc(xsq_ready, 1)
            act.wait_ge(consts_ready, 1)
            act.wait_ge(ssq_ready, 1)
            nc.scalar.activation(rms[:, :], bank[7][:, 0:SEQ], ACT.Sqrt, scale=1.0 / D_MODEL,
                                 bias=eps[:, :]).then_inc(rms_ready, 1)
            act.wait_ge(half_ready, 16)
            nc.scalar.activation(w_hi[:, 0, 0:HALF], slot(*SPLIT[0])[:, 0:HALF], ACT.Copy).then_inc(half_hi, 1)
            arrived(act, *SPLIT[0])
            nc.scalar.activation(w_hi[:, 0, HALF:], slot(*SPLIT[0])[:, HALF:], ACT.Copy).then_inc(hi_done, 1)
            act.wait_ge(xhat_ready, 1)
            act.wait_ge(mod_cols_read, 2)
            for k in range(KT):
                nc.scalar.activation(act_hi[:, k, :], xt[:, k, :], ACT.Identity, scale=scale[:, 0, k:k + 1],
                                     bias=shift[:, 0, k:k + 1]).then_inc(xn_hi, 1)
            split_hi(1)

            def conv_gate(j):
                act.wait_ge(w_used, SP_AT["conv", j] + 1)
                if j >= 2:
                    act.wait_ge(glu_ready, j - 1)
                nc.scalar.activation(glu_gate[:, j % 2, :], bank[j % 2][:, 0:SEQ], ACT.Sigmoid).then_inc(sig_ready, 1)
                sigs[0] += 1

            def qk_raw_out(j):
                act.wait_ge(w_used, SP_AT["qk", j] + 1)
                nc.scalar.activation(qk[:, j, :], bank[j % 2][:, :], ACT.Copy).then_inc(qk_raw, 1)
                if j >= 2:
                    act.wait_ge(qk_ssq, j - 1)
                nc.scalar.activation(qk_sq[:, j % 2, :], bank[j % 2][:, :], ACT.Square).then_inc(qk_sq_ready, 1)

            def after(m):
                kind, i = SPLIT[m]
                if kind == "conv":
                    conv_gate(i)
                elif kind == "qk":
                    qk_raw_out(i)
                    if i == CT - 1:
                        act.wait_ge(qk_ssq, CT)
                        nc.scalar.activation(qk_stat[:, :], bank[6][:, 0:ST * 16], ACT.Sqrt, scale=1.0 / HEAD_DIM,
                                             bias=eps[:, :]).then_inc(qk_std, 1)

            done_mults, sigs = [0], [0]

            def mults(count):
                for n in range(done_mults[0], min(done_mults[0] + count, len(MULTS))):
                    j, i = MULTS[n]
                    if sigs[0] <= j:
                        return
                    w = col("conv_w", j * CONV_TAPS + i)
                    if i == 0:
                        act.wait_ge(glu_ready, j + 1)
                        nc.scalar.activation(conv[:, j, :], glu[:, j, 0:SEQ], ACT.Identity, scale=w,
                                             bias=col("conv_b", j)).then_inc(tap_mult, 1)
                    else:
                        if n >= KT:
                            act.wait_ge(pool_tap, sum(k > 0 for _, k in MULTS[:n - KT + 1]))
                        nc.scalar.activation(tap_prod(n), glu[:, j, i:i + SEQ], ACT.Copy, scale=w).then_inc(tap_mult, 1)
                    done_mults[0] = n + 1

            for m in range(SP_AT["v", 1] + 1):
                if m >= 1:
                    after(m - 1)
                mults(MULTS_PER_STEP // 2)
                if m + 2 <= SP_AT["v", 1]:
                    split_hi(m + 2)
                mults(MULTS_PER_STEP - MULTS_PER_STEP // 2)
            mults(len(MULTS))
            def exps(h):
                for t, (a, b, _) in enumerate(ROWS):
                    n = 2 * h + t
                    act.wait_ge(peaked, h + 1)
                    nc.scalar.activation(prob[:, h % 3, a:b], prob[:, h % 3, a:b], ACT.Exp, bias=npeak[:, n:n + 1],
                                         accum_out=total[:, n:n + 1]).then_inc(exped, 1)

            def turn_copy(h):
                act.wait_ge(turned, h + 1)
                if h >= 2:
                    act.wait_ge(attended, h - 1)
                nc.scalar.activation(prob_t[:, h % 2, :], bank[2][:, 0:384], ACT.Copy).then_inc(turned_copied, 1)

            def att_hi_part(j):
                act.wait_ge(attended, 2 * j + 2)
                nc.scalar.activation(act_hi[:, j, :], bank[3][:, 0:SEQ], ACT.Copy).then_inc(att_hi, 1)

            def gn_deviation():
                act.wait_ge(gn_ssq, 1)
                nc.scalar.activation(gn_stat[:, :], bank[6][:, 0:ST * 8], ACT.Sqrt, scale=1.0 / 64,
                                     bias=eps[:, :]).then_inc(gn_std, 1)

            def gn_swish():
                for j in range(CT):
                    act.wait_ge(gn_scaled, j + 1)
                    nc.scalar.activation(xmod[:, CT + j, :], conv[:, j, :], ACT.Silu, bias=col("gn_b", j)).then_inc(gn_silu, 1)

            nc.scalar.activation(half2[:, 0:1], eps[:, :], ACT.Exp)
            act.wait_ge(w_used, SP_AT["v", 1] + 1)
            for t in range(ST):
                nc.scalar.activation(v[:, t, :], bank[4 + t][:, :], ACT.Copy).then_inc(v_ready, 1)
            exps(0)
            for h in range(HEADS):
                if h + 1 < HEADS:
                    exps(h + 1)
                turn_copy(h)
                if h == 1:
                    gn_deviation()
                elif h == 3:
                    gn_swish()
                if h % 2 == 0 and h >= 2:
                    att_hi_part(h // 2 - 1)
                if h in HIGH_AT_HEAD:
                    split_hi(HIGH_AT_HEAD[h])
            att_hi_part(CT - 1)
            nc.scalar.activation(half2[:, 0:1], eps[:, :], ACT.Sqrt)
            split_hi(SP_AT["up", 1])
            for i in range(2 * ST):
                act.wait_ge(x2_right if i % 2 else x2_left, i // 2 + 1)
                nc.scalar.activation(xmod[:, 2 * i:2 * i + 2, :].rearrange("p a b -> p (a b)"),
                                     xr[:, i // 2, (i % 2) * 512:(i % 2) * 512 + 512], ACT.Square,
                                     accum_out=ssq2[:, i:i + 1]).then_inc(x2_sq, 1)
                t = i // 2
                if i % 2 == 0:
                    act.wait_ge(x2_sq, i + 1)
                    nc.scalar.activation(half2[:, t:t + 1], ssq2[:, i:i + 1], ACT.Identity, scale=1.0 / D_MODEL,
                                         bias=eps[:, :]).then_inc(x2_half, 1)
                else:
                    act.wait_ge(x2_sq, i + 1)
                    act.wait_ge(x2_half, t + 1)
                    nc.scalar.activation(rms2[:, t:t + 1], ssq2[:, i:i + 1], ACT.Sqrt, scale=1.0 / D_MODEL,
                                         bias=half2[:, t:t + 1]).then_inc(x2_std, 1)
            for n in range(2):
                act.wait_ge(gate_bc, n + 3)
                nc.scalar.activation(gate[:, 1, n * 512:n * 512 + 512], bank[4 + n][:, :], ACT.Copy).then_inc(gate2_ready, 1)
            for k in range(KT):
                act.wait_ge(x2_turned, k - k % 2 + 2)
                nc.scalar.activation(xt[:, k, :], bank[k // 2][:, (k % 2) * SEQ:(k % 2) * SEQ + SEQ], ACT.Identity,
                                     scale=scale[:, 1, k:k + 1], bias=shift[:, 1, k:k + 1]).then_inc(xn2_full, 1)
            split_hi(SP_AT["up", 2])

            def tap_two(t):
                act.wait_ge(w_used, SP_AT["up", t] + 1)
                if t >= 2:
                    act.wait_ge(hidden, t - 1)
                for g in range(2):
                    nc.scalar.activation(ug[:, t % 2, g, :], bank[4 + 2 * (t % 2) + g][:, 0:SEQ], ACT.Identity,
                                         scale=col("ffn_w", (g * FT + t) * FFN_TAPS + 2),
                                         bias=col("ffn_b", g * FT + t)).then_inc(tap2, 1)

            def gate_silu(t):
                act.wait_ge(tap0, 2 * t + 2)
                nc.scalar.activation(silu_g[:, t % 2, :], ug[:, t % 2, 1, :], ACT.Silu).then_inc(gated, 1)

            def hid_high(t):
                act.wait_ge(hidden, t + 1)
                if t >= 4:
                    act.wait_ge(w_used, SP_AT["down", t // 2 - 2] + 1)
                nc.scalar.activation(hid_hi[:, t % 4, :], hid[:, t % 2, :], ACT.Copy).then_inc(hid_hi_ready, 1)

            m0 = SP_AT["up", 0]
            for m in range(m0, len(SPLIT)):
                done = m > m0 and SPLIT[m - 1][0] == "up"
                if done:
                    tap_two(SPLIT[m - 1][1])
                if m > m0:
                    split_hi(m + 2)
                if done:
                    gate_silu(SPLIT[m - 1][1])
                    hid_high(SPLIT[m - 1][1])

        @block.vector
        def _(dve):
            def split_lo(m):
                if m >= len(SPLIT):
                    return
                dve.wait_ge(hi_done, m + 1)
                arrived(dve, *SPLIT[m])
                if m >= PARTS:
                    dve.wait_ge(w_used, m - PARTS + 1)
                nc.vector.tensor_tensor(w_lo[:, m % PARTS, :], slot(*SPLIT[m]),
                                        w_hi[:, m % PARTS, :].bitcast(f32), ALU.subtract).then_inc(lo_done, 1)

            dve.wait_ge(rms_ready, 1)
            nc.vector.reciprocal(rinv[:, :], rms[:, :]).then_inc(rinv_ready, 1)
            dve.wait_ge(rinv_ready, 1)
            dve.wait_ge(xt_ready, 16)
            for k in range(KT):
                last = nc.vector.tensor_tensor(xt[:, k, :], xt[:, k, :], rinv[:, :], ALU.mult)
            last.then_inc(xhat_ready, 1)
            nc.vector.tensor_scalar(q_gain[:, :], col("q_g"), HEAD_DIM ** -0.5, None, ALU.mult)

            def xn_low(k):
                dve.wait_ge(xn_full, k + 1)
                dve.wait_ge(xn_hi, k + 1)
                nc.vector.tensor_tensor(act_lo[:, k, :], xmod[:, k, :], act_hi[:, k, :].bitcast(f32),
                                        ALU.subtract).then_inc(xn_lo, 1)

            def mod_rows_out(which):
                dve.wait_ge(mod_done, 1 + 2 * which)
                nc.vector.tensor_copy(mod_rows[:, :], bank[7 * which][:, :]).then_inc(mod_rows_ready, 1)

            def mod_columns(which, gain, shift_b, scale_b):
                dve.wait_ge(mod_cols_ready, which + 1)
                turned_rows = bank[1 if which == 0 else 4][:, :].rearrange("p (j q r) -> p q j r", j=4, q=4)
                nc.vector.tensor_tensor(shift[:, which, :].rearrange("p (q j) -> p q j", q=2), turned_rows[:, 0:2, :, 0],
                                        cols_of(shift_b).rearrange("p (q j) -> p q j", q=2), ALU.add)
                nc.vector.tensor_tensor(scale[:, which, :].rearrange("p (q j) -> p q j", q=2), turned_rows[:, 2:4, :, 0],
                                        cols_of(scale_b).rearrange("p (q j) -> p q j", q=2), ALU.add).then_inc(mod_cols_read, 1)
                dve.wait_ge(mod_cols_read, 2 * which + 1)
                nc.vector.scalar_tensor_tensor(scale[:, which, :], scale[:, which, :], 1.0, cols_of(gain), ALU.add,
                                               ALU.mult).then_inc(mod_cols_read, 1)
                dve.wait_ge(mod_cols_read, 2 * which + 2)

            mod_rows_out(0)
            dve.wait_ge(half_ready, 16)
            dve.wait_ge(half_hi, 1)
            nc.vector.tensor_tensor(w_lo[:, 0, 0:HALF], slot(*SPLIT[0])[:, 0:HALF],
                                    w_hi[:, 0, 0:HALF].bitcast(f32), ALU.subtract).then_inc(half_lo, 1)
            mod_columns(0, "norm1_g", "sh1_b", "sc1_b")
            dve.wait_ge(xhat_ready, 1)
            for k in range(KT):
                if k == POOL_LOWS:
                    arrived(dve, *SPLIT[0])
                    dve.wait_ge(hi_done, 1)
                    nc.vector.tensor_tensor(w_lo[:, 0, HALF:], slot(*SPLIT[0])[:, HALF:],
                                            w_hi[:, 0, HALF:].bitcast(f32), ALU.subtract).then_inc(lo_done, 1)
                nc.vector.tensor_scalar(xmod[:, k, :], xt[:, k, :], scale[:, 0, k:k + 1], shift[:, 0, k:k + 1],
                                        ALU.mult, ALU.add).then_inc(xn_full, 1)
                if k > POOL_LOWS:
                    xn_low(k - 1)
            xn_low(KT - 1)
            split_lo(1)

            done_taps, glus = [0], [0]

            def taps(n):
                for n_tap in range(done_taps[0], min(done_taps[0] + n, len(TAPS))):
                    j, i = TAPS[n_tap]
                    if glus[0] <= j:
                        return
                    w = col("conv_w", j * CONV_TAPS + i)
                    if i == 0:
                        dve.wait_ge(glu_ready, j + 1)
                        nc.vector.tensor_scalar(conv[:, j, :], glu[:, j, 0:SEQ], w, col("conv_b", j), ALU.mult,
                                                ALU.add).then_inc(tap, 1)
                    else:
                        dve.wait_ge(tap, TAPS.index((j, i - 1)) + 1)
                        nc.vector.scalar_tensor_tensor(conv[:, j, :], glu[:, j, i:i + SEQ], w, conv[:, j, :],
                                                       ALU.mult, ALU.add).then_inc(tap, 1)
                    done_taps[0] = n_tap + 1

            def after(m):
                kind, j = SPLIT[m]
                if kind == "conv":
                    dve.wait_ge(sig_ready, j + 1)
                    nc.vector.tensor_tensor(glu[:, j, CONV_TAPS - 1:], bank[j % 2][:, SEQ:2 * SEQ],
                                            glu_gate[:, j % 2, :], ALU.mult).then_inc(glu_ready, 1)
                    glus[0] += 1

            dve.wait_ge(consts_ready, 1)
            for m in range(SP_AT["v", 0] + 1):
                if m >= 1:
                    after(m - 1)
                if m + 2 <= SP_AT["v", 1]:
                    split_lo(m + 2)
                if 2 <= m < SP_AT["v", 0]:
                    taps(8 if m < SP_AT["qk", 0] else 10)
            def gn_centre(g):
                dve.wait_ge(gn_mean, g + 1)
                dve.wait_ge(tap, PAIR_TAPS[g])
                dve.wait_ge(pool_tap, (g + 1) * (CONV_TAPS - 1))
                both = conv[:, 2 * g:2 * g + 2, :].rearrange("p a b -> p (a b)")
                nc.vector.tensor_tensor(both, both, bank[GN_BANK[g]][:, :], ALU.subtract).then_inc(gn_centred, 1)

            def gn_scale():
                dve.wait_ge(gn_sq, 2)
                for j in range(CT):
                    dve.wait_ge(gn_bc, j // 2 + 1)
                    half = slice((j % 2) * SEQ, (j % 2) * SEQ + SEQ)
                    nc.vector.scalar_tensor_tensor(conv[:, j, :], conv[:, j, :], col("gn_g", j),
                                                   bank[GN_BANK[j // 2]][:, half], ALU.mult, ALU.mult).then_inc(gn_scaled, 1)

            def mix_parts():
                for j in range(CT):
                    dve.wait_ge(gn_silu, j + 1)
                    nc.vector.tensor_copy(act_hi[:, CT + j, :], xmod[:, CT + j, :]).then_inc(mix_hi, 1)
                for j in range(CT):
                    dve.wait_ge(mix_hi, j + 1)
                    nc.vector.tensor_tensor(act_lo[:, CT + j, :], xmod[:, CT + j, :], act_hi[:, CT + j, :].bitcast(f32),
                                            ALU.subtract).then_inc(mix_lo, 1)

            def qk_normalise(j):
                dve.wait_ge(qk_bc, j + 1)
                dve.wait_ge(qk_raw, j + 1)
                for part, gain in enumerate((q_gain[:, :], col("k_g"))):
                    cut = slice(part * SEQ, (part + 1) * SEQ)
                    nc.vector.scalar_tensor_tensor(qk[:, j, cut], qk[:, j, cut], gain, bank[j % 2][:, cut], ALU.mult,
                                                   ALU.mult).then_inc(qk_normed, 1)

            dve.wait_ge(qk_std, 1)
            nc.vector.reciprocal(qk_inv[:, :], qk_stat[:, :]).then_inc(qk_inverted, 1)
            taps(4)
            dve.wait_ge(qk_turned, 1)
            nc.vector.tensor_copy(qk_rstd[:, :], bank[6][0:16, SEQ:2 * SEQ]).then_inc(qk_rs, 1)
            taps(len(TAPS))
            qk_normalise(0)
            qk_normalise(1)
            dve.wait_ge(mod_done, 2)
            dve.wait_ge(gates_b_ready, 16)
            nc.vector.tensor_tensor(gates_b[:, :], bank[2][:, :], gates_b[:, :], ALU.add).then_inc(mod_rows_ready, 1)
            qk_normalise(2)
            qk_normalise(3)

            def add_bias(h):
                dve.wait_ge(scores, h + 1)
                if h >= 3:
                    dve.wait_ge(turned, h - 2)
                for t, (a, b, c) in enumerate(ROWS):
                    n = 2 * h + t
                    nc.vector.tensor_tensor_reduce(prob[:, h % 3, a:b], bank[h % 2][:, a:b], bias[:, h, SEQ - 1 - c::-1],
                                                   1.0, 2 * NEG, ALU.add, ALU.max, peak[:, n:n + 1]).then_inc(biased, 1)
                dve.wait_ge(biased, 2 * h + 2)
                nc.vector.tensor_scalar(npeak[:, 2 * h:2 * h + 2], peak[:, 2 * h:2 * h + 2], -1.0, None,
                                        ALU.mult).then_inc(peaked, 1)

            def normalise(h):
                dve.wait_ge(exped, 2 * h + 2)
                nc.vector.reciprocal(rtotal[:, 2 * h:2 * h + 2], total[:, 2 * h:2 * h + 2]).then_inc(inverted, 1)
                dve.wait_ge(inverted, h + 1)
                for t, (a, b, _) in enumerate(ROWS):
                    n = 2 * h + t
                    last = nc.vector.tensor_scalar(prob[:, h % 3, a:b], prob[:, h % 3, a:b], rtotal[:, n:n + 1], None,
                                                   ALU.mult)
                last.then_inc(normed, 1)

            def att_lo_part(j):
                dve.wait_ge(att_hi, j + 1)
                nc.vector.tensor_tensor(act_lo[:, j, :], bank[3][:, 0:SEQ], act_hi[:, j, :].bitcast(f32),
                                        ALU.subtract).then_inc(att_lo, 1)

            dve.wait_ge(bias_ready, 16)
            add_bias(0)
            add_bias(1)
            for h in range(HEADS):
                normalise(h)
                if h == 0:
                    gn_centre(0)
                    gn_centre(1)
                elif h + 1 < HEADS:
                    add_bias(h + 1)
                if h in (1, 2):
                    dve.wait_ge(gate_bc, h)
                    nc.vector.tensor_copy(gate[:, 0, h * 512 - 512:h * 512], bank[4][:, :]).then_inc(gate_ready, 1)
                if h == 2:
                    dve.wait_ge(gn_std, 1)
                    nc.vector.reciprocal(gn_inv[:, :], gn_stat[:, :]).then_inc(gn_inverted, 1)
                    mod_rows_out(1)
                elif h == 3:
                    dve.wait_ge(gn_turned, 1)
                    nc.vector.tensor_copy(gn_rstd[:, :], bank[6][0:8, SEQ:2 * SEQ]).then_inc(gn_rs, 1)
                    mod_columns(1, "norm2_g", "sh2_b", "sc2_b")
                    gn_scale()
                elif h == 4:
                    mix_parts()
                if h in LOW_AT_HEAD:
                    split_lo(LOW_AT_HEAD[h])
                if h % 2 == 0 and h >= 2:
                    att_lo_part(h // 2 - 1)
            att_lo_part(CT - 1)
            dve.wait_ge(xr_ready, 16)

            def x2_diagonal(t):
                dve.wait_ge(x2_std, t + 1)
                nc.vector.reciprocal(rinv2[:, t:t + 1], rms2[:, t:t + 1]).then_inc(x2_rs, 1)
                dve.wait_ge(x2_rs, t + 1)
                nc.vector.tensor_scalar(diag[:, t, :], ident[:, :], rinv2[:, t:t + 1], None, ALU.mult).then_inc(x2_diag, 1)

            def gated_mixer(i):
                half = slice((i % 2) * 512, (i % 2) * 512 + 512)
                dve.wait_ge(mixed, i + 1)
                nc.vector.tensor_tensor(tmp[:, i, :], bank[OUT_BANK + i][:, :], gate[:, 0, half], ALU.mult).then_inc(x2_part, 1)

            for t in range(ST):
                gated_mixer(2 * t)
                gated_mixer(2 * t + 1)
                dve.wait_ge(x2_part, 2 * t + 2)
                nc.vector.tensor_tensor(xr[:, t, 512:], xr[:, t, 512:], tmp[:, 2 * t + 1, :], ALU.add).then_inc(x2_right, 1)
            x2_diagonal(0)
            x2_diagonal(1)
            for k in range(KT):
                dve.wait_ge(xn2_full, k + 1)
                nc.vector.tensor_copy(act_hi[:, k, :], xt[:, k, :]).then_inc(xn2_hi, 1)
                if k % 2 == 1:
                    dve.wait_ge(xn2_hi, k)
                    nc.vector.tensor_tensor(act_lo[:, k - 1, :], xt[:, k - 1, :], act_hi[:, k - 1, :].bitcast(f32),
                                            ALU.subtract).then_inc(xn2_lo, 1)
            split_lo(SP_AT["up", 1])

            def earlier_taps(t):
                for g in range(2):
                    dve.wait_ge(tap2, 2 * t + g + 1)
                    nc.vector.scalar_tensor_tensor(ug[:, t % 2, g, 1:], bank[4 + 2 * (t % 2) + g][:, 0:SEQ - 1],
                                                   col("ffn_w", (g * FT + t) * FFN_TAPS + 1), ug[:, t % 2, g, 1:],
                                                   ALU.mult, ALU.add).then_inc(tap1, 1)
                for g in range(2):
                    dve.wait_ge(tap1, 2 * t + g + 1)
                    nc.vector.scalar_tensor_tensor(ug[:, t % 2, g, 2:], bank[4 + 2 * (t % 2) + g][:, 0:SEQ - 2],
                                                   col("ffn_w", (g * FT + t) * FFN_TAPS), ug[:, t % 2, g, 2:],
                                                   ALU.mult, ALU.add).then_inc(tap0, 1)

            def gate_hidden(t):
                dve.wait_ge(gated, t + 1)
                if t >= 2:
                    dve.wait_ge(hid_lo_ready, t - 1)
                nc.vector.tensor_tensor(hid[:, t % 2, :], ug[:, t % 2, 0, :], silu_g[:, t % 2, :],
                                        ALU.mult).then_inc(hidden, 1)

            def hid_low(t):
                dve.wait_ge(hid_hi_ready, t + 1)
                if t >= 4:
                    dve.wait_ge(w_used, SP_AT["down", t // 2 - 2] + 1)
                nc.vector.tensor_tensor(hid_lo[:, t % 4, :], hid[:, t % 2, :], hid_hi[:, t % 4, :].bitcast(f32),
                                        ALU.subtract).then_inc(hid_lo_ready, 1)

            m0 = SP_AT["up", 0]
            for m in range(m0, len(SPLIT)):
                done = m > m0 and SPLIT[m - 1][0] == "up"
                if done:
                    earlier_taps(SPLIT[m - 1][1])
                split_lo(m + 2)
                if done:
                    gate_hidden(SPLIT[m - 1][1])
                    hid_low(SPLIT[m - 1][1])
            dve.wait_ge(gate2_ready, 2)
            for t in range(ST):
                for n in range(2):
                    i = 2 * t + n
                    dve.wait_ge(down_done, i + 1)
                    cut = slice(n * 512, (n + 1) * 512)
                    if i >= 2:
                        dve.wait_ge(out_ready, i - 1)
                    nc.vector.tensor_tensor(tmp[:, i % 2, :], bank[i][:, :], gate[:, 1, cut], ALU.mult).then_inc(out_part, 1)
                    dve.wait_ge(out_part, i + 1)
                    nc.vector.tensor_tensor(xmod[:, 4 * t + 2 * n:4 * t + 2 * n + 2, :].rearrange("p a b -> p (a b)"),
                                            xr[:, t, cut], tmp[:, i % 2, :], ALU.add).then_inc(out_ready, 1)

        @block.tensor
        def _(pe):
            def product(o, stat, mov, first, last):
                (sh, sl), (mh, ml) = stat, mov
                nc.tensor.matmul(o, sh, mh, start=first, stop=False)
                nc.tensor.matmul(o, sh, ml, start=False, stop=False)
                return nc.tensor.matmul(o, sl, mh, start=False, stop=last)

            def weights(m, a, n):
                hi, lo = parts(m)
                return hi[:, a:a + n], lo[:, a:a + n]

            def acts(k, a, n):
                return act_hi[:, k, a:a + n], act_lo[:, k, a:a + n]

            def ready(m):
                pe.wait_ge(lo_done, m + 1)
                pe.wait_ge(hi_done, m + 1)

            def ada(n, to):
                arrived(pe, "ada", n)
                k = n % KT
                for q in range(4):
                    last = nc.tensor.matmul(bank[to][32 * q:32 * q + 32, :], silu_c[:, k:k + 1].to_broadcast([P, 32]),
                                            slot("ada", n)[:, 512 * q:512 * q + 512], start=(k == 0), stop=(k == KT - 1))
                last.then_inc(ada_used, 1)

            def ada_end(groups):
                pe.wait_ge(ada_used, groups * KT)
                nc.tensor.transpose(bank[(6, 7, 5)[groups - 1]][:, SEQ:SEQ + P], ident[:, :], ident[:, :]).then_inc(mod_done, 1)

            def turn_mod_rows(to):
                for j in range(4):
                    last = nc.tensor.transpose(bank[to][:, j * P:(j + 1) * P], mod_rows[:, j * P:(j + 1) * P], ident[:, :])
                last.then_inc(mod_cols_ready, 1)

            def keep_clock(n):
                for _ in range(n):
                    nc.tensor.transpose(bank[2][:, 0:P], ident[:, :], ident[:, :])

            pe.wait_ge(consts_ready, 1)
            pe.wait_ge(xsq_ready, 1)
            for k in range(KT):
                last = nc.tensor.matmul(bank[7][:, 0:SEQ], ones[:, :], xmod[:, k, :], start=(k == 0), stop=(k == KT - 1))
            last.then_inc(ssq_ready, 1)
            pe.wait_ge(silu_c_ready, 1)
            for k in range(KT):
                if k == KT - 1:
                    keep_clock(8)
                ada(k, 0)
            ada_end(1)
            keep_clock(4)
            pe.wait_ge(mod_rows_ready, 1)
            turn_mod_rows(1)
            keep_clock(14)

            def pair(m, to):
                for c in range(2):
                    for k in range(KT):
                        if m == 0 and c == 0 and k == 0:
                            pe.wait_ge(half_lo, 1)
                            pe.wait_ge(half_hi, 1)
                        elif m == 0 and c == 0 and k == KT // 2:
                            ready(0)
                        if m == 0 and c == 0:
                            pe.wait_ge(xn_hi, k + 1)
                            if k < POOL_LOWS:
                                pe.wait_ge(xn_lo_pool, k + 1)
                            else:
                                pe.wait_ge(xn_lo, k - POOL_LOWS + 1)
                        last = product(bank[to][:, c * SEQ:(c + 1) * SEQ], weights(m, k * 2 * P + c * P, P),
                                       acts(k, 0, SEQ), k == 0, k == KT - 1)
                last.then_inc(w_used, 1)

            ada_at = [KT]

            def later_ada(after):
                for _ in range(ADA_AFTER.get(after, 0)):
                    ada(ada_at[0], 2)
                    ada_at[0] += 1

            pe.wait_ge(mod_cols_read, 2)
            for j in range(CT):
                m = SP_AT["conv", j]
                if j > 0:
                    ready(m)
                if j >= 2:
                    pe.wait_ge(glu_ready, j - 1)
                pair(m, j % 2)
                later_ada(("conv", j))

            def qk_squares(j):
                pe.wait_ge(qk_sq_ready, j + 1)
                for t in range(ST):
                    for part in range(2):
                        a = t * 16 + part * 8 + 2 * j
                        last = nc.tensor.matmul(bank[6][:, a:a + 2],
                                                qk_sq[:, j % 2, part * SEQ + t * P:part * SEQ + (t + 1) * P],
                                                to_group[:, 0, 0:2], start=True, stop=True)
                last.then_inc(qk_ssq, 1)

            def qk_turn():
                pe.wait_ge(qk_inverted, 1)
                for t in range(ST):
                    last = nc.tensor.transpose(bank[6][0:16, SEQ + t * P:SEQ + (t + 1) * P],
                                               qk_inv[:, t * 16:(t + 1) * 16], ident[:, :])
                last.then_inc(qk_turned, 1)

            for j in range(CT):
                m = SP_AT["qk", j]
                ready(m)
                if j < 2:
                    pe.wait_ge(glu_ready, CT - 1 + j)
                else:
                    pe.wait_ge(qk_sq_ready, j - 1)
                pair(m, j % 2)
                if j >= 1:
                    qk_squares(j - 1)
                later_ada(("qk", j))

            def qk_spread(j):
                pe.wait_ge(qk_rs, 1)
                if j >= 2:
                    pe.wait_ge(qk_normed, 2 * (j - 1))
                else:
                    pe.wait_ge(qk_sq_ready, CT)
                for part in range(2):
                    last = nc.tensor.matmul(bank[j % 2][:, part * SEQ:(part + 1) * SEQ], from_group[:, 4 * part + j, :],
                                            qk_rstd[:, :], start=True, stop=True)
                last.then_inc(qk_bc, 1)

            def gn_means(g):
                pe.wait_ge(tap, PAIR_TAPS[g])
                pe.wait_ge(pool_tap, (g + 1) * (CONV_TAPS - 1))
                for c in range(2):
                    last = nc.tensor.matmul(bank[GN_BANK[g]][:, c * SEQ:(c + 1) * SEQ], half_mean[:, :],
                                            conv[:, 2 * g + c, :], start=True, stop=True)
                last.then_inc(gn_mean, 1)

            def gn_squares():
                for c in range(CT):
                    pe.wait_ge(gn_sq, c // 2 + 1)
                    for t in range(ST):
                        a = t * 8 + 2 * c
                        last = nc.tensor.matmul(bank[6][:, a:a + 2], xmod[:, c, t * P:(t + 1) * P],
                                                to_group[:, 0, 0:2], start=True, stop=True)
                last.then_inc(gn_ssq, 1)

            def gn_turn():
                pe.wait_ge(gn_inverted, 1)
                for t in range(ST):
                    last = nc.tensor.transpose(bank[6][0:8, SEQ + t * P:SEQ + (t + 1) * P], gn_inv[:, t * 8:(t + 1) * 8],
                                               ident[:, :])
                last.then_inc(gn_turned, 1)

            def gn_spread():
                pe.wait_ge(gn_rs, 1)
                for c in range(CT):
                    last = nc.tensor.matmul(bank[GN_BANK[c // 2]][:, (c % 2) * SEQ:(c % 2) * SEQ + SEQ],
                                            from_group[0:8, c, :], gn_rstd[:, :], start=True, stop=True)
                    if c % 2 == 1:
                        last.then_inc(gn_bc, 1)

            def v_half(i, t):
                m = SP_AT["v", i]
                ready(m)
                for k in range(KT // 2):
                    kk = i * KT // 2 + k
                    last = product(bank[4 + t][:, :], acts(kk, t * P, P), weights(m, k * 512, 512),
                                   kk == 0, kk == KT - 1)
                return last

            def late_ada(n):
                for _ in range(n):
                    ada(ada_at[0], 2 if ada_at[0] < 2 * KT else 7)
                    ada_at[0] += 1
                    if ada_at[0] == 2 * KT:
                        ada_end(2)

            v_half(0, 0)
            qk_squares(CT - 1)
            v_half(0, 1).then_inc(w_used, 1)
            qk_turn()
            if ada_at[0] == 2 * KT:
                ada_end(2)
            late_ada(2)
            qk_spread(0)
            qk_spread(1)
            v_half(1, 0)
            late_ada(1)
            qk_spread(2)
            qk_spread(3)
            v_half(1, 1).then_inc(w_used, 1)

            def head_scores(h):
                j, r = h // 2, slice(64 * (h % 2), 64 * (h % 2) + 64)
                pe.wait_ge(qk_normed, max(2 * (j + 1), 2 * CT if h < 2 else 0))
                if h >= 2:
                    pe.wait_ge(biased, 2 * (h - 1))
                for t, (a, b, _) in enumerate(ROWS):
                    last = nc.tensor.matmul(bank[h % 2][:, a:b], qk[r, j, t * P:(t + 1) * P], qk[r, j, SEQ:SEQ + b - a],
                                            start=True, stop=True)
                last.then_inc(scores, 1)

            def head_turn(h):
                pe.wait_ge(normed, h + 1)
                if h >= 1:
                    pe.wait_ge(turned_copied, h)
                for t in range(3):
                    last = nc.tensor.transpose(bank[2][:, t * P:(t + 1) * P], prob[:, h % 3, t * P:(t + 1) * P],
                                               ident[:, :])
                last.then_inc(turned, 1)

            def head_values(h):
                pe.wait_ge(turned_copied, h + 1)
                r = slice(64 * (h % 2), 64 * (h % 2) + 64)
                if h % 2 == 0 and h >= 2:
                    pe.wait_ge(att_lo, h // 2)
                nc.tensor.matmul(bank[3][r, 0:SEQ], v[:, 0, h * 64:(h + 1) * 64], prob_t[:, h % 2, 0:SEQ],
                                 start=True, stop=False)
                nc.tensor.matmul(bank[3][r, P:SEQ], v[:, 1, h * 64:(h + 1) * 64], prob_t[:, h % 2, SEQ:384],
                                 start=False, stop=True).then_inc(attended, 1)

            def spread_gate(n):
                nc.tensor.matmul(bank[4 if n < 2 else 2 + n][:, :], ones[32 * n:32 * n + 1, :],
                                 gates_b[32 * n:32 * n + 1, :], start=True, stop=True,
                                 tile_position=(32 * n, 0)).then_inc(gate_bc, 1)

            def out_part(i, banks=range(2 * ST)):
                m, k = SP_AT["out", i // 2], OUT_TILES[i]
                ready(m)
                if k >= CT:
                    pe.wait_ge(mix_lo, k - CT + 1)
                else:
                    pe.wait_ge(att_lo, k + 1)
                for b in banks:
                    t, n = b // 2, b % 2
                    last = product(bank[OUT_BANK + b][:, :], acts(k, t * P, P),
                                   weights(m, (i % 2) * D_MODEL + n * 512, 512), i == 0, i == KT - 1)
                return last

            head_scores(0)
            head_scores(1)
            gn_means(0)
            pe.wait_ge(v_ready, ST)
            gn_means(1)
            for h in range(HEADS):
                if 1 < h + 1 < HEADS:
                    head_scores(h + 1)
                head_turn(h)
                if h == 0:
                    spread_gate(0)
                elif h == 1:
                    gn_squares()
                elif h == 2:
                    pe.wait_ge(gate_ready, 1)
                    spread_gate(1)
                elif h == 3:
                    pe.wait_ge(mod_rows_ready, 3)
                    pe.wait_ge(gate_ready, 2)
                    turn_mod_rows(4)
                    gn_spread()
                elif h == 4:
                    pe.wait_ge(mod_cols_read, 4)
                    pe.wait_ge(gn_scaled, CT)
                    out_part(0)
                elif h == 5:
                    out_part(1).then_inc(w_used, 1)
                    out_part(2)
                elif h == 6:
                    out_part(3).then_inc(w_used, 1)
                    out_part(4)
                else:
                    out_part(5).then_inc(w_used, 1)
                if h < len(ADA_AT_HEAD):
                    late_ada(ADA_AT_HEAD[h])
                    if h == len(ADA_AT_HEAD) - 1:
                        ada_end(3)
                head_values(h)
                if h == 2:
                    gn_turn()
            out_part(6)
            for b in range(2 * ST):
                last = out_part(7, [b])
                last.then_inc(mixed, 1)
            nc.tensor.transpose(bank[3][:, 0:P], ident[:, :], ident[:, :]).then_inc(w_used, 1)
            for n in range(2):
                pe.wait_ge(x2_part, n + 1)
                spread_gate(2 + n)
            pe.wait_ge(biased, 2 * HEADS)
            pe.wait_ge(att_lo, CT)
            for t in range(ST):
                pe.wait_ge(x2_diag, t + 1)
                pe.wait_ge(x2_left, t + 1)
                pe.wait_ge(x2_right, t + 1)
                for k in range(KT):
                    last = nc.tensor.matmul(bank[k // 2][:, (k % 2) * SEQ + t * P:(k % 2) * SEQ + (t + 1) * P],
                                            xr[:, t, k * P:(k + 1) * P], diag[:, t, :], start=True, stop=True)
                    if t == ST - 1:
                        last.then_inc(x2_turned, 1)

            def up(t):
                m = SP_AT["up", t]
                ready(m)
                if t == 0:
                    pe.wait_ge(gate2_ready, 2)
                elif t == 1:
                    pe.wait_ge(x2_part, 2 * ST)
                if t >= 2:
                    pe.wait_ge(tap0, 2 * (t - 1))
                for g in range(2):
                    for k in range(KT):
                        if t == 0 and g == 0:
                            pe.wait_ge(xn2_lo_pool if k % 2 else xn2_lo, k // 2 + 1)
                        last = product(bank[4 + 2 * (t % 2) + g][:, 0:SEQ], weights(m, k * 2 * P + g * P, P),
                                       acts(k, 0, SEQ), k == 0, k == KT - 1)
                last.then_inc(w_used, 1)

            def down(i):
                m = SP_AT["down", i]
                ready(m)
                pe.wait_ge(hid_lo_ready, 2 * i + 2)
                pe.wait_ge(hid_hi_ready, 2 * i + 2)
                order = [(f, b) for f in range(2) for b in range(2 * ST)] if i < FT // 2 - 1 else \
                        [(f, b) for b in range(2 * ST) for f in range(2)]
                for f, b in order:
                    t, n = b // 2, b % 2
                    place = (2 * i + f) % 4
                    h = (hid_hi[:, place, t * P:(t + 1) * P], hid_lo[:, place, t * P:(t + 1) * P])
                    last = product(bank[b][:, :], h, weights(m, f * D_MODEL + n * 512, 512),
                                   i == 0 and f == 0, i == FT // 2 - 1 and f == 1)
                    if i == FT // 2 - 1 and f == 1:
                        last.then_inc(down_done, 1)
                if i < FT // 2 - 1:
                    last.then_inc(w_used, 1)

            for kind, i in UP_DOWN:
                (up if kind == "up" else down)(i)


def _layout(x, c, rel_bias, ada_w, ada_b, norm1_g, w_in, q_norm_g, k_norm_g, conv_dw_w, conv_dw_b, conv_norm_g,
            conv_norm_b, w_out, norm2_g, w_up, ffn_dw_w, ffn_dw_b, w_down):
    a = {k: np.asarray(v) for k, v in locals().items()}

    def by_tile(v):
        return v.reshape(-1, P).T

    def pairs(w, first, second, n):
        w = w.reshape(KT, P, -1, P)
        return [np.stack([w[:, :, first + j], w[:, :, second + j]], 2).transpose(1, 0, 2, 3).reshape(P, SLOT)
                for j in range(n)]

    ada = a["ada_w"][0].reshape(KT, P, 12, 512)
    w_in = a["w_in"][0]
    slots = {}
    for g, chunks in enumerate(ADA_GROUPS):
        for k in range(KT):
            slots["ada", g * KT + k] = ada[k][:, list(chunks)].reshape(P, SLOT)
    for j, s in enumerate(pairs(w_in, 16, 12, CT)):
        slots["conv", j] = s
    for j, s in enumerate(pairs(w_in, 0, 4, CT)):
        slots["qk", j] = s
    wv = w_in[:, 1024:1536].reshape(2, KT // 2, P, 512)
    for i in range(2):
        slots["v", i] = wv[i].transpose(1, 0, 2).reshape(P, SLOT)
    wo = a["w_out"][0].reshape(KT, P, D_MODEL).transpose(1, 0, 2)
    for j in range(4):
        slots["out", j] = wo[:, OUT_TILES[2 * j:2 * j + 2]].reshape(P, SLOT)
    for t, s in enumerate(pairs(a["w_up"][0], 0, FT, FT)):
        slots["up", t] = s
    wd = a["w_down"][0].reshape(FT // 2, 2, P, D_MODEL)
    for i in range(FT // 2):
        slots["down", i] = wd[i].transpose(1, 0, 2).reshape(P, SLOT)
    stream = np.stack([slots[s] for s in STREAM])

    b = a["ada_b"][0].reshape(6, D_MODEL)
    parts = {
        "c": by_tile(a["c"][0]), "norm1_g": by_tile(a["norm1_g"][0]), "norm2_g": by_tile(a["norm2_g"][0]),
        "sh1_b": by_tile(b[0]), "sc1_b": by_tile(b[1]), "sh2_b": by_tile(b[3]), "sc2_b": by_tile(b[4]),
        "conv_w": a["conv_dw_w"][0].reshape(CONV_TAPS, CT, P).transpose(2, 1, 0).reshape(P, -1),
        "conv_b": by_tile(a["conv_dw_b"][0]), "gn_g": by_tile(a["conv_norm_g"][0]), "gn_b": by_tile(a["conv_norm_b"][0]),
        "ffn_w": a["ffn_dw_w"][0].reshape(FFN_TAPS, 2 * FT, P).transpose(2, 1, 0).reshape(P, -1),
        "ffn_b": by_tile(a["ffn_dw_b"][0]),
        "q_g": np.tile(a["q_norm_g"][0], 2)[:, None], "k_g": np.tile(a["k_norm_g"][0], 2)[:, None],
    }
    cols = np.concatenate([parts[k] for k in COLS], axis=1)
    x2 = a["x"][0]
    return {
        "stream": stream,
        "x_t": x2.T.reshape(KT, P, SEQ).transpose(1, 0, 2),
        "x_rows": x2.reshape(ST, P, D_MODEL).transpose(1, 0, 2),
        "cols": cols,
        "ada_b_gates": np.repeat(a["ada_b"][0].reshape(12, 512)[list(ADA_GROUPS[1])], 32, axis=0),
        "rel_bias": a["rel_bias"],
    }


def kernel(**inputs):
    import concourse.bacc as _bacc
    from concourse.bass_utils import run_bass_kernel_spmd as _run

    nc = _bacc.Bacc("TRN2", target_bir_lowering=False, num_devices=1)
    arrays, args = {}, []
    for name, a in _layout(**inputs).items():
        a = np.ascontiguousarray(a)
        arrays[f"in_{name}"] = a
        args.append(nc.dram_tensor(f"in_{name}", a.shape, mybir.dt.from_np(a.dtype), kind="ExternalInput").ap())
    out = nc.dram_tensor("out_0", (ST, P, D_MODEL), mybir.dt.float32, kind="ExternalOutput").ap()
    hymba_layer(nc, *args, out)
    r = _run(nc, [arrays], core_ids=[0])
    return r.results[0]["out_0"].reshape(1, SEQ, D_MODEL)
```

```python
import math
from contextlib import ExitStack

import numpy as np

import concourse.bass as bass
from concourse import mybir

D_MODEL, SEQ = 1024, 256
HEADS, HEAD_DIM = 8, 64
CONV_TAPS, FFN_TAPS = 31, 3
FFN_HIDDEN = 2816
N_BUCKETS, MAX_DISTANCE = 32, 1024
EPS, NEG = 1e-6, -1e30

P = 128
KT = D_MODEL // P
ST = SEQ // P
CT = D_MODEL // 2 // P
FT = FFN_HIDDEN // P
SLOT = 2048

ADA_GROUPS = [(0, 1, 2, 3), (4, 5, 10, 11), (6, 7, 8, 9)]
PRODUCTS_AFTER = {3: (0,), 4: (1, 2), 5: (3,), 6: (4,), 7: (5,), 8: (6, 7)}
HIGH_AFTER = {2: (0,), 3: (1, 2), 4: (3,), 5: (4,), 6: (5,), 7: (6,), 8: (7,)}
UP_DOWN = [("up", 0), ("up", 1)]
for _i in range(FT // 2):
    if _i + 1 < FT // 2:
        UP_DOWN += [("up", 2 * _i + 2), ("up", 2 * _i + 3)]
    UP_DOWN += [("down", _i)]
ADA_AFTER = {("conv", 2): 1, ("conv", 3): 1, ("qk", 0): 1, ("qk", 1): 1, ("qk", 2): 1, ("qk", 3): 2}
ADA_AT_HEAD = (2, 2, 1)
FIRST = 2
STREAM = [("ada", 0), ("ada", 1), ("conv", 0), ("ada", 2), ("conv", 1),
          ("ada", 3), ("ada", 4), ("ada", 5), ("ada", 6), ("ada", 7), ("conv", 2)]
_ada = KT
for _s in [("conv", j) for j in range(FIRST, CT)] + [("qk", j) for j in range(CT)] + [("v", 0), ("v", 1)]:
    if _s not in STREAM:
        STREAM.append(_s)
    for _ in range(ADA_AFTER.get(_s, 0)):
        STREAM.append(("ada", _ada))
        _ada += 1
ADA_LATE = range(_ada, 3 * KT)
STREAM += [("ada", n) for n in ADA_LATE] + [("out", j) for j in range(4)] + UP_DOWN
OUT_TILES = [0, 1, 4, 5, 6, 7, 2, 3]
SPLIT = [x for x in STREAM if x[0] != "ada"]
AT = {x: n for n, x in enumerate(STREAM)}
SP_AT = {x: m for m, x in enumerate(SPLIT)}
RAW, PARTS = 6, 3

COLS = {}
_at = 0
for _name, _n in [("c", KT), ("norm1_g", KT), ("norm2_g", KT), ("sh1_b", KT), ("sc1_b", KT), ("sh2_b", KT),
                  ("sc2_b", KT), ("conv_w", CT * CONV_TAPS), ("conv_b", CT), ("gn_g", CT), ("gn_b", CT),
                  ("ffn_w", 2 * FT * FFN_TAPS), ("ffn_b", 2 * FT), ("q_g", 1), ("k_g", 1)]:
    COLS[_name] = (_at, _n)
    _at += _n
N_COLS = _at

LEAD = 20
TAPS = [(1, i) for i in range(LEAD)]
TAPS += [(t, i - LEAD * (t == 3)) for i in range(LEAD, CONV_TAPS) for t in (1, 3)]
TAPS += [(3, i) for i in range(CONV_TAPS - LEAD, CONV_TAPS)]
PAIR_TAPS = (TAPS.index((1, CONV_TAPS - 1)) + 1, len(TAPS))
MULTS = [(t, i) for t in (0, 2) for i in range(CONV_TAPS)]
MULTS_PER_STEP = 6


def bucket_ranges():
    d = np.arange(SEQ)
    exact = N_BUCKETS // 2
    nf = np.maximum(d, 1).astype(np.float32)
    large = exact + (np.log(nf / np.float32(exact)) / np.float32(math.log(MAX_DISTANCE / exact))
                     * np.float32(N_BUCKETS - exact)).astype(np.int32)
    b = np.where(d < exact, d, np.minimum(large, N_BUCKETS - 1))
    return [(int(v), int(d[b == v][0]), int(d[b == v][-1])) for v in np.unique(b)]


def hymba_layer(nc, stream, x_t, x_rows, cols_in, ada_b_gates, rel_bias, out):
    f32, f32r = mybir.dt.float32, mybir.dt.float32r
    ALU, ACT = mybir.AluOpType, mybir.ActivationFunctionType

    toeplitz_rows = nc.dram_tensor("toeplitz_rows", [HEADS, 384], f32, kind="Internal").ap()

    ctx = ExitStack()
    with ctx:
        def sb(name, shape, dt=f32):
            return ctx.enter_context(nc.sbuf_tensor(name, shape, dt))

        def sem(name):
            return ctx.enter_context(nc.semaphore(name))

        bank = [ctx.enter_context(nc.psum_tensor(f"bank{i}", [P, 512], f32)) for i in range(8)]

        raw = sb("raw", [P, RAW, SLOT])
        w_hi = sb("w_hi", [P, PARTS, SLOT], f32r)
        w_lo = sb("w_lo", [P, PARTS, SLOT], f32r)
        xt = sb("xt", [P, KT, SEQ])
        xmod = sb("xmod", [P, KT, SEQ])
        act_hi = sb("act_hi", [P, KT, SEQ], f32r)
        act_lo = sb("act_lo", [P, KT, SEQ], f32r)
        xr = sb("xr", [P, ST, D_MODEL])
        gate = sb("gate", [P, 2, D_MODEL])
        cols = sb("cols", [P, N_COLS])
        silu_c = sb("silu_c", [P, KT])
        gates_b = sb("gates_b", [P, 512])
        mod_rows = sb("mod_rows", [P, 512])
        scale = sb("scale", [P, 2, KT])
        shift = sb("shift", [P, 2, KT])
        rms = sb("rms", [P, SEQ])
        rinv = sb("rinv", [P, SEQ])
        ident = sb("ident", [P, P])
        ones = sb("ones", [P, P])
        half_mean = sb("half_mean", [P, P])
        to_group = sb("to_group", [P, 8, 16])
        from_group = sb("from_group", [16, 8, P])
        pick = sb("pick", [P, 1])
        table = sb("table", [HEADS, N_BUCKETS])
        bias_rows = sb("bias_rows", [HEADS, 384])
        bias = sb("bias", [P, HEADS, SEQ])
        glu_gate = sb("glu_gate", [P, 2, SEQ])
        glu = sb("glu", [P, CT, SEQ + CONV_TAPS - 1])
        conv = sb("conv", [P, CT, SEQ])
        gn_stat = sb("gn_stat", [P, ST * 8])
        gn_inv = sb("gn_inv", [P, ST * 8])
        gn_rstd = sb("gn_rstd", [8, SEQ])
        qk = sb("qk", [P, CT, 2 * SEQ])
        qk_sq = gate[:, 0, :].rearrange("p (a b) -> p a b", a=2)
        qk_stat = sb("qk_stat", [P, ST * 16])
        qk_inv = sb("qk_inv", [P, ST * 16])
        qk_rstd = sb("qk_rstd", [16, SEQ])
        q_gain = sb("q_gain", [P, 1])
        v = gate[:, 1, :].rearrange("p (t n) -> p t n", t=ST)
        prob = sb("prob", [P, 3, 384])
        prob_t = sb("prob_t", [P, 2, 384])
        peak = sb("peak", [P, 2 * HEADS])
        npeak = sb("npeak", [P, 2 * HEADS])
        total = sb("total", [P, 2 * HEADS])
        rtotal = sb("rtotal", [P, 2 * HEADS])
        ssq2 = sb("ssq2", [P, 2 * ST])
        half2 = sb("half2", [P, ST])
        diag = sb("diag", [P, ST, P])
        rms2 = sb("rms2", [P, ST])
        rinv2 = sb("rinv2", [P, ST])
        tmp = qk
        ug = bias[:, 0:4, :].rearrange("p (t g) s -> p t g s", t=2)
        silu_g = bias[:, 4:6, :]
        hid = bias[:, 6:8, :]
        out_rows = xmod[:, :, :].rearrange("p (i a) b -> p i (a b)", i=2 * ST)
        hid_hi = sb("hid_hi", [P, 4, SEQ], f32r)
        hid_lo = sb("hid_lo", [P, 4, SEQ], f32r)
        eps = sb("eps", [P, 1])

        raw_ready = [sem(f"raw_ready{i}") for i in range(RAW)]
        cols_ready, xt_ready, xr_ready = sem("cols_ready"), sem("xt_ready"), sem("xr_ready")
        gates_b_ready, table_ready = sem("gates_b_ready"), sem("table_ready")
        rows_stored, bias_ready = sem("rows_stored"), sem("bias_ready")
        norm1_copied, norm1_turned, norm1_read, norm1_scale = (
            sem(s) for s in ("norm1_copied", "norm1_turned", "norm1_read", "norm1_scale"))
        pool_step, consts_ready = sem("pool_step"), sem("consts_ready")
        ada_used, w_used = sem("ada_used"), sem("w_used")
        hi_done, lo_done = sem("hi_done"), sem("lo_done")
        silu_c_ready, xsq_ready, ssq_ready, rms_ready = (sem(s) for s in ("silu_c_ready", "xsq_ready", "ssq_ready", "rms_ready"))
        mod_done, mod_rows_ready, mod_cols_ready = sem("mod_done"), sem("mod_rows_ready"), sem("mod_cols_ready")
        mod_cols_read = sem("mod_cols_read")
        gate_bc, gate_ready, gate2_ready = sem("gate_bc"), sem("gate_ready"), sem("gate2_ready")
        xn_full, xn_hi, xn_lo, xn_lo_pool = (sem(s) for s in ("xn_full", "xn_hi", "xn_lo", "xn_lo_pool"))
        sig_ready, glu_ready = sem("sig_ready"), sem("glu_ready")
        tap, tap_mult, pool_tap = sem("tap"), sem("tap_mult"), sem("pool_tap")
        qk_raw, qk_sq_ready, qk_ssq, qk_std, qk_inverted, qk_turned, qk_rs, qk_bc, qk_normed = (
            sem(s) for s in ("qk_raw", "qk_sq_ready", "qk_ssq", "qk_std", "qk_inverted", "qk_turned", "qk_rs", "qk_bc", "qk_normed"))
        v_ready, rinv_ready, xhat_ready, mixed = sem("v_ready"), sem("rinv_ready"), sem("xhat_ready"), sem("mixed")
        scores, biased, peaked, exped, inverted, normed, turned, turned_copied, attended, att_hi, att_lo = (
            sem(s) for s in ("scores", "biased", "peaked", "exped", "inverted", "normed", "turned", "turned_copied",
                             "attended", "att_hi", "att_lo"))
        gn_mean, gn_centred, gn_sq, gn_ssq, gn_std, gn_inverted, gn_turned, gn_rs, gn_bc, gn_scaled, gn_silu, mix_hi, mix_lo = (
            sem(s) for s in ("gn_mean", "gn_centred", "gn_sq", "gn_ssq", "gn_std", "gn_inverted", "gn_turned", "gn_rs", "gn_bc", "gn_scaled",
                             "gn_silu", "mix_hi", "mix_lo"))
        x2_part, x2_left, x2_right, x2_sq, x2_sq_last, x2_half, x2_std, x2_rs, x2_diag, x2_turned, xn2_full, xn2_hi, xn2_lo, xn2_lo_pool = (
            sem(s) for s in ("x2_part", "x2_left", "x2_right", "x2_sq", "x2_sq_last", "x2_half", "x2_std", "x2_rs", "x2_diag", "x2_turned",
                             "xn2_full", "xn2_hi", "xn2_lo", "xn2_lo_pool"))
        tap2, tap1, tap0, gated, hidden, hid_hi_ready, hid_lo_ready, down_done = (
            sem(s) for s in ("tap2", "tap1", "tap0", "gated", "hidden", "hid_hi_ready", "hid_lo_ready", "down_done"))
        out_part, out_ready, out_left, stored = sem("out_part"), sem("out_ready"), sem("out_left"), sem("stored")

        def col(name, i=0):
            a, _ = COLS[name]
            return cols[:, a + i:a + i + 1]

        def cols_of(name):
            a, n = COLS[name]
            return cols[:, a:a + n]

        def slot(kind, i):
            return raw[:, AT[kind, i] % RAW, :]

        def arrived(eng, kind, i):
            n = AT[kind, i]
            eng.wait_ge(raw_ready[n % RAW], 16 * (n // RAW + 1))

        def parts(m):
            return w_hi[:, m % PARTS, :], w_lo[:, m % PARTS, :]

        def tap_prod(n):
            return xmod[:, n % KT, :]

        POOL_LOWS = 5

        ROWS = [(0, P, P), (P, 384, 0)]
        GN_BANK = (6, 5)
        OUT_BANK = 4

        HIGH_AT_HEAD = {0: SP_AT["out", 0], 2: SP_AT["out", 1], 4: SP_AT["out", 2], 5: SP_AT["out", 3], 6: SP_AT["up", 0]}
        LOW_AT_HEAD = {1: SP_AT["out", 0], 4: SP_AT["out", 1], 5: SP_AT["out", 2], 6: SP_AT["out", 3], 7: SP_AT["up", 0]}

        block = ctx.enter_context(nc.Block())

        @block.sync
        def _(sp):
            sp.dma_start(cols[:, :], cols_in).then_inc(cols_ready, 16)
            sp.dma_start(xt[:, :, :], x_t).then_inc(xt_ready, 16)
            for n, (kind, i) in enumerate(STREAM):
                if n >= RAW:
                    k0, i0 = STREAM[n - RAW]
                    if k0 == "ada":
                        sp.wait_ge(ada_used, i0 + 1)
                    else:
                        sp.wait_ge(lo_done, SP_AT[k0, i0] + 1)
                sp.dma_start(raw[:, n % RAW, :], stream[n]).then_inc(raw_ready[n % RAW], 16)
                if (kind, i) == ("v", 1):
                    sp.wait_ge(rows_stored, 16)
                    sp.dma_start(bias[:, :, :], bass.AP(toeplitz_rows.tensor, 0, [[1, P], [384, HEADS], [1, SEQ]])
                                 ).then_inc(bias_ready, 16)
                if (kind, i) == ("qk", 3):
                    sp.dma_start(gates_b[:, :], ada_b_gates).then_inc(gates_b_ready, 16)
                if (kind, i) == ("up", 0):
                    sp.dma_start(xr[:, :, :], x_rows).then_inc(xr_ready, 16)
            for i in range(2 * ST - 1):
                sp.wait_ge(out_ready, i + 1)
                sp.dma_start(out[i // 2, :, (i % 2) * 512:(i % 2) * 512 + 512], out_rows[:, i, :]).then_inc(stored, 16)
            sp.wait_ge(out_left, 1)
            sp.dma_start(out[ST - 1, :, 512:768], out_rows[:, 2 * ST - 1, 0:256]).then_inc(stored, 16)
            sp.wait_ge(stored, 16 * (2 * ST + 1))

        @block.gpsimd
        def _(pool):
            step = [0]

            def chained(ins):
                step[0] += 1
                ins.then_inc(pool_step, 1)
                pool.wait_ge(pool_step, step[0])

            pool.dma_start(table[:, :], rel_bias).then_inc(table_ready, 16)
            chained(nc.gpsimd.memset(eps[:, :], EPS))
            chained(nc.gpsimd.memset(ones[:, :], 1.0))
            chained(nc.gpsimd.memset(half_mean[:, :], 0.0))
            chained(nc.gpsimd.memset(glu[:, :, 0:CONV_TAPS - 1], 0.0))
            chained(nc.gpsimd.memset(from_group[:, :, :], 0.0))
            chained(nc.gpsimd.memset(to_group[:, :, :], 0.0))
            chained(nc.gpsimd.memset(ident[:, :], 0.0))
            chained(nc.gpsimd.memset(pick[:, :], 0.0))
            for q in range(4):
                chained(nc.gpsimd.memset(pick[32 * q:32 * q + 1, :], 1.0))
            flat = to_group[:, :, :].rearrange("p j m -> p (j m)")
            for half in range(2):
                rows = slice(64 * half, 64 * half + 64)
                chained(nc.gpsimd.memset(flat[rows, half:128:18], 1.0))
                chained(nc.gpsimd.memset(half_mean[rows, rows], 1.0 / 64))
            chained(nc.gpsimd.affine_select(out=ident[:, :], in_=ident[:, :], compare_op=ALU.not_equal, fill=1.0,
                                            base=0, pattern=[[-1, P]], channel_multiplier=1))
            wide = from_group[:, :, :].rearrange("p j (a c) -> p j a c", a=2)
            nc.gpsimd.affine_select(out=wide, in_=wide, compare_op=ALU.not_equal, fill=1.0, base=0,
                                    pattern=[[-2, 8], [-1, 2], [0, 64]], channel_multiplier=1).then_inc(consts_ready, 1)
            pool.wait_ge(table_ready, 16)
            chained(nc.gpsimd.memset(bias_rows[:, 0:P - 1], NEG))
            chained(nc.gpsimd.memset(bias_rows[:, 383:384], NEG))
            for b, lo, hi in bucket_ranges():
                n = hi - lo + 1
                chained(nc.gpsimd.tensor_copy(bias_rows[:, P - 1 + lo:P + hi],
                                              table[:, b:b + 1].to_broadcast([HEADS, n])))
            pool.dma_start(toeplitz_rows, bias_rows[:, :]).then_inc(rows_stored, 16)
            for k in range(POOL_LOWS):
                pool.wait_ge(xn_full, k + 1)
                pool.wait_ge(xn_hi, k + 1)
                nc.gpsimd.tensor_tensor(act_lo[:, k, :], xmod[:, k, :], act_hi[:, k, :].bitcast(f32),
                                        ALU.subtract).then_inc(xn_lo_pool, 1)
            added = 0
            for n, (j, i) in enumerate(MULTS):
                if i == 0:
                    continue
                pool.wait_ge(tap_mult, n + 1)
                if i >= 2:
                    pool.wait_ge(pool_tap, added)
                nc.gpsimd.tensor_tensor(conv[:, j, :], conv[:, j, :], tap_prod(n), ALU.add).then_inc(pool_tap, 1)
                added += 1
            for g in range(2):
                pool.wait_ge(gn_centred, g + 1)
                if g == 1:
                    pool.wait_ge(pool_tap, len(MULTS) - 2)
                nc.gpsimd.tensor_tensor(xmod[:, 2 * g:2 * g + 2, :], conv[:, 2 * g:2 * g + 2, :],
                                        conv[:, 2 * g:2 * g + 2, :], ALU.mult).then_inc(gn_sq, 1)
            pool.wait_ge(xr_ready, 16)
            for t in range(ST):
                pool.wait_ge(x2_part, 2 * t + 1)
                nc.gpsimd.tensor_tensor(xr[:, t, 0:512], xr[:, t, 0:512], tmp[:, 2 * t, :], ALU.add).then_inc(x2_left, 1)
            for k in range(1, KT, 2):
                pool.wait_ge(xn2_hi, k + 1)
                nc.gpsimd.tensor_tensor(act_lo[:, k, :], xt[:, k, :], act_hi[:, k, :].bitcast(f32),
                                        ALU.subtract).then_inc(xn2_lo_pool, 1)

            pool.wait_ge(out_part, 2 * ST)
            nc.gpsimd.tensor_tensor(out_rows[:, 2 * ST - 1, 0:256], xr[:, ST - 1, 512:768], tmp[:, 1, 0:256],
                                    ALU.add).then_inc(out_left, 1)

        @block.scalar
        def _(act):
            def split_hi(m):
                if m >= len(SPLIT):
                    return
                arrived(act, *SPLIT[m])
                if m >= PARTS:
                    act.wait_ge(w_used, m - PARTS + 1)
                nc.scalar.activation(w_hi[:, m % PARTS, :], slot(*SPLIT[m]), ACT.Copy).then_inc(hi_done, 1)

            act.wait_ge(cols_ready, 16)
            nc.scalar.activation(silu_c[:, :], cols_of("c"), ACT.Silu).then_inc(silu_c_ready, 1)
            act.wait_ge(xt_ready, 16)
            nc.scalar.activation(xmod[:, :, :], xt[:, :, :], ACT.Square).then_inc(xsq_ready, 1)
            def copy_rows(k):
                act.wait_ge(ada_used, k + 1)
                if k >= 2:
                    act.wait_ge(norm1_turned, k - 1)
                nc.scalar.activation(mod_rows[:, (k % 2) * 2 * P:(k % 2 + 1) * 2 * P], bank[2 + k % 2][:, 0:2 * P],
                                     ACT.Copy).then_inc(norm1_copied, 1)

            split_hi(0)
            copy_rows(0)
            act.wait_ge(consts_ready, 1)
            act.wait_ge(ssq_ready, 1)
            nc.scalar.activation(rms[:, :], bank[7][:, 0:SEQ], ACT.Sqrt, scale=1.0 / D_MODEL,
                                 bias=eps[:, :]).then_inc(rms_ready, 1)
            copy_rows(1)

            def xn_high(k):
                act.wait_ge(xhat_ready, k + 1)
                act.wait_ge(norm1_scale, k + 1)
                nc.scalar.activation(act_hi[:, k, :], xt[:, k, :], ACT.Identity, scale=scale[:, 0, k:k + 1],
                                     bias=shift[:, 0, k:k + 1]).then_inc(xn_hi, 1)

            for k in range(2, KT + 1):
                if k < KT:
                    if k == 99:
                        split_hi(FIRST)
                    copy_rows(k)
                if k == 2:
                    split_hi(1)
                if k == 8:
                    split_hi(FIRST)
                for tile in HIGH_AFTER[k]:
                    xn_high(tile)

            def conv_gate(j):
                act.wait_ge(w_used, SP_AT["conv", j] + 1)
                if j >= 2:
                    act.wait_ge(glu_ready, j - 1)
                nc.scalar.activation(glu_gate[:, j % 2, :], bank[j % 2][:, 0:SEQ], ACT.Sigmoid).then_inc(sig_ready, 1)
                sigs[0] += 1

            def qk_raw_out(j):
                act.wait_ge(w_used, SP_AT["qk", j] + 1)
                nc.scalar.activation(qk[:, j, :], bank[j % 2][:, :], ACT.Copy).then_inc(qk_raw, 1)
                if j >= 2:
                    act.wait_ge(qk_ssq, j - 1)
                nc.scalar.activation(qk_sq[:, j % 2, :], bank[j % 2][:, :], ACT.Square).then_inc(qk_sq_ready, 1)

            def after(m):
                kind, i = SPLIT[m]
                if kind == "conv":
                    conv_gate(i)
                elif kind == "qk":
                    qk_raw_out(i)
                    if i == CT - 1:
                        act.wait_ge(qk_ssq, CT)
                        nc.scalar.activation(qk_stat[:, :], bank[6][:, 0:ST * 16], ACT.Sqrt, scale=1.0 / HEAD_DIM,
                                             bias=eps[:, :]).then_inc(qk_std, 1)

            done_mults, sigs = [0], [0]

            def mults(count):
                for n in range(done_mults[0], min(done_mults[0] + count, len(MULTS))):
                    j, i = MULTS[n]
                    if sigs[0] <= j:
                        return
                    w = col("conv_w", j * CONV_TAPS + i)
                    if i == 0:
                        act.wait_ge(glu_ready, j + 1)
                        nc.scalar.activation(conv[:, j, :], glu[:, j, 0:SEQ], ACT.Identity, scale=w,
                                             bias=col("conv_b", j)).then_inc(tap_mult, 1)
                    else:
                        if n >= KT:
                            act.wait_ge(pool_tap, sum(k > 0 for _, k in MULTS[:n - KT + 1]))
                        nc.scalar.activation(tap_prod(n), glu[:, j, i:i + SEQ], ACT.Copy, scale=w).then_inc(tap_mult, 1)
                    done_mults[0] = n + 1

            for m in range(SP_AT["v", 1] + 1):
                if m >= 1:
                    after(m - 1)
                mults(MULTS_PER_STEP // 2)
                if 1 <= m <= SP_AT["v", 1] - 2:
                    split_hi(m + 2)
                mults(MULTS_PER_STEP - MULTS_PER_STEP // 2)
            mults(len(MULTS))

            def exps(h):
                for t, (a, b, _) in enumerate(ROWS):
                    n = 2 * h + t
                    act.wait_ge(peaked, h + 1)
                    nc.scalar.activation(prob[:, h % 3, a:b], prob[:, h % 3, a:b], ACT.Exp, bias=npeak[:, n:n + 1],
                                         accum_out=total[:, n:n + 1]).then_inc(exped, 1)

            def turn_copy(h):
                act.wait_ge(turned, h + 1)
                if h >= 2:
                    act.wait_ge(attended, h - 1)
                nc.scalar.activation(prob_t[:, h % 2, :], bank[2][:, 0:384], ACT.Copy).then_inc(turned_copied, 1)

            def att_hi_part(j):
                act.wait_ge(attended, 2 * j + 2)
                nc.scalar.activation(act_hi[:, j, :], bank[3][:, 0:SEQ], ACT.Copy).then_inc(att_hi, 1)

            def gn_deviation():
                act.wait_ge(gn_ssq, 1)
                nc.scalar.activation(gn_stat[:, :], bank[6][:, 0:ST * 8], ACT.Sqrt, scale=1.0 / 64,
                                     bias=eps[:, :]).then_inc(gn_std, 1)

            def gn_swish():
                for j in range(CT):
                    act.wait_ge(gn_scaled, j + 1)
                    nc.scalar.activation(xmod[:, CT + j, :], conv[:, j, :], ACT.Silu, bias=col("gn_b", j)).then_inc(gn_silu, 1)

            nc.scalar.activation(half2[:, 0:1], eps[:, :], ACT.Exp)
            act.wait_ge(w_used, SP_AT["v", 1] + 1)
            for t in range(ST):
                nc.scalar.activation(v[:, t, :], bank[4 + t][:, :], ACT.Copy).then_inc(v_ready, 1)
            exps(0)
            for h in range(HEADS):
                if h % 2 == 0 and h >= 2:
                    att_hi_part(h // 2 - 1)
                if h + 1 < HEADS:
                    exps(h + 1)
                turn_copy(h)
                if h == 1:
                    gn_deviation()
                if h == 4:
                    gn_swish()
                if h in HIGH_AT_HEAD:
                    split_hi(HIGH_AT_HEAD[h])
            att_hi_part(CT - 1)
            nc.scalar.activation(half2[:, 0:1], eps[:, :], ACT.Sqrt)
            split_hi(SP_AT["up", 1])
            for i in range(2 * ST):
                t = i // 2
                if i == 2 * ST - 1:
                    act.wait_ge(x2_half, t + 1)
                    act.wait_ge(x2_sq_last, 1)
                    nc.scalar.activation(rms2[:, t:t + 1], ssq2[:, i:i + 1], ACT.Sqrt, scale=1.0 / D_MODEL,
                                         bias=half2[:, t:t + 1]).then_inc(x2_std, 1)
                    break
                act.wait_ge(x2_right if i % 2 else x2_left, i // 2 + 1)
                nc.scalar.activation(xmod[:, 2 * i:2 * i + 2, :].rearrange("p a b -> p (a b)"),
                                     xr[:, i // 2, (i % 2) * 512:(i % 2) * 512 + 512], ACT.Square,
                                     accum_out=ssq2[:, i:i + 1]).then_inc(x2_sq, 1)
                if i % 2 == 0:
                    act.wait_ge(x2_sq, i + 1)
                    nc.scalar.activation(half2[:, t:t + 1], ssq2[:, i:i + 1], ACT.Identity, scale=1.0 / D_MODEL,
                                         bias=eps[:, :]).then_inc(x2_half, 1)
                else:
                    act.wait_ge(x2_sq, i + 1)
                    act.wait_ge(x2_half, t + 1)
                    nc.scalar.activation(rms2[:, t:t + 1], ssq2[:, i:i + 1], ACT.Sqrt, scale=1.0 / D_MODEL,
                                         bias=half2[:, t:t + 1]).then_inc(x2_std, 1)
            for n in range(2):
                act.wait_ge(gate_bc, n + 3)
                nc.scalar.activation(gate[:, 1, n * 512:n * 512 + 512], bank[4 + n][:, :], ACT.Copy).then_inc(gate2_ready, 1)
            for k in range(KT):
                act.wait_ge(x2_turned, k - k % 2 + 2)
                nc.scalar.activation(xt[:, k, :], bank[k // 2][:, (k % 2) * SEQ:(k % 2) * SEQ + SEQ], ACT.Identity,
                                     scale=scale[:, 1, k:k + 1], bias=shift[:, 1, k:k + 1]).then_inc(xn2_full, 1)
            split_hi(SP_AT["up", 2])

            def tap_two(t):
                act.wait_ge(w_used, SP_AT["up", t] + 1)
                if t >= 2:
                    act.wait_ge(hidden, t - 1)
                for g in range(2):
                    nc.scalar.activation(ug[:, t % 2, g, :], bank[4 + 2 * (t % 2) + g][:, 0:SEQ], ACT.Identity,
                                         scale=col("ffn_w", (g * FT + t) * FFN_TAPS + 2),
                                         bias=col("ffn_b", g * FT + t)).then_inc(tap2, 1)

            def gate_silu(t):
                act.wait_ge(tap0, 2 * t + 2)
                nc.scalar.activation(silu_g[:, t % 2, :], ug[:, t % 2, 1, :], ACT.Silu).then_inc(gated, 1)

            def hid_high(t):
                act.wait_ge(hidden, t + 1)
                if t >= 4:
                    act.wait_ge(w_used, SP_AT["down", t // 2 - 2] + 1)
                nc.scalar.activation(hid_hi[:, t % 4, :], hid[:, t % 2, :], ACT.Copy).then_inc(hid_hi_ready, 1)

            m0 = SP_AT["up", 0]
            for m in range(m0, len(SPLIT)):
                done = m > m0 and SPLIT[m - 1][0] == "up"
                if done:
                    tap_two(SPLIT[m - 1][1])
                if m > m0:
                    split_hi(m + 2)
                if done:
                    gate_silu(SPLIT[m - 1][1])
                    hid_high(SPLIT[m - 1][1])
            act.wait_ge(out_ready, 2 * ST)
            act.dma_start(out[ST - 1, :, 768:], out_rows[:, 2 * ST - 1, 256:]).then_inc(stored, 16)

        @block.vector
        def _(dve):
            def split_lo(m):
                if m >= len(SPLIT):
                    return
                dve.wait_ge(hi_done, m + 1)
                arrived(dve, *SPLIT[m])
                if m >= PARTS:
                    dve.wait_ge(w_used, m - PARTS + 1)
                nc.vector.tensor_tensor(w_lo[:, m % PARTS, :], slot(*SPLIT[m]),
                                        w_hi[:, m % PARTS, :].bitcast(f32), ALU.subtract).then_inc(lo_done, 1)

            split_lo(0)
            dve.wait_ge(rms_ready, 1)
            nc.vector.reciprocal(rinv[:, :], rms[:, :]).then_inc(rinv_ready, 1)
            dve.wait_ge(rinv_ready, 1)
            dve.wait_ge(xt_ready, 16)
            nc.vector.tensor_scalar(q_gain[:, :], col("q_g"), HEAD_DIM ** -0.5, None, ALU.mult)

            def xn_low(k):
                dve.wait_ge(xn_full, k + 1)
                dve.wait_ge(xn_hi, k + 1)
                nc.vector.tensor_tensor(act_lo[:, k, :], xmod[:, k, :], act_hi[:, k, :].bitcast(f32),
                                        ALU.subtract).then_inc(xn_lo, 1)

            def norm1_columns(k):
                dve.wait_ge(norm1_turned, k + 1)
                columns = bank[6 + k % 2]
                nc.vector.tensor_tensor(shift[:, 0, k:k + 1], columns[:, 2 * k:2 * k + 1], col("sh1_b", k), ALU.add)
                nc.vector.tensor_tensor(scale[:, 0, k:k + 1], columns[:, 2 * k + 1:2 * k + 2], col("sc1_b", k),
                                        ALU.add).then_inc(norm1_read, 1)
                dve.wait_ge(norm1_read, k + 1)
                nc.vector.scalar_tensor_tensor(scale[:, 0, k:k + 1], scale[:, 0, k:k + 1], 1.0, col("norm1_g", k), ALU.add,
                                               ALU.mult).then_inc(norm1_scale, 1)
                dve.wait_ge(norm1_scale, k + 1)

            def mod_rows_out():
                dve.wait_ge(mod_done, 2)
                nc.vector.tensor_copy(mod_rows[:, :], bank[7][:, :]).then_inc(mod_rows_ready, 1)

            def norm2_columns():
                dve.wait_ge(mod_cols_ready, 1)
                turned_rows = bank[4][:, :].rearrange("p (j q r) -> p q j r", j=4, q=4)
                nc.vector.tensor_tensor(shift[:, 1, :].rearrange("p (q j) -> p q j", q=2), turned_rows[:, 0:2, :, 0],
                                        cols_of("sh2_b").rearrange("p (q j) -> p q j", q=2), ALU.add)
                nc.vector.tensor_tensor(scale[:, 1, :].rearrange("p (q j) -> p q j", q=2), turned_rows[:, 2:4, :, 0],
                                        cols_of("sc2_b").rearrange("p (q j) -> p q j", q=2), ALU.add).then_inc(mod_cols_read, 1)
                dve.wait_ge(mod_cols_read, 1)
                nc.vector.scalar_tensor_tensor(scale[:, 1, :], scale[:, 1, :], 1.0, cols_of("norm2_g"), ALU.add,
                                               ALU.mult).then_inc(mod_cols_read, 1)
                dve.wait_ge(mod_cols_read, 2)

            for k in range(KT):
                nc.vector.tensor_tensor(xt[:, k, :], xt[:, k, :], rinv[:, :], ALU.mult).then_inc(xhat_ready, 1)
                norm1_columns(k)
                dve.wait_ge(xhat_ready, k + 1)
                nc.vector.tensor_scalar(xmod[:, k, :], xt[:, k, :], scale[:, 0, k:k + 1], shift[:, 0, k:k + 1],
                                        ALU.mult, ALU.add).then_inc(xn_full, 1)
                if k >= POOL_LOWS:
                    xn_low(k)
                if k == 1:
                    split_lo(1)
                elif k == 7:
                    split_lo(FIRST)

            done_taps, glus = [0], [0]

            def taps(n):
                for n_tap in range(done_taps[0], min(done_taps[0] + n, len(TAPS))):
                    j, i = TAPS[n_tap]
                    if glus[0] <= j:
                        return
                    w = col("conv_w", j * CONV_TAPS + i)
                    if i == 0:
                        dve.wait_ge(glu_ready, j + 1)
                        nc.vector.tensor_scalar(conv[:, j, :], glu[:, j, 0:SEQ], w, col("conv_b", j), ALU.mult,
                                                ALU.add).then_inc(tap, 1)
                    else:
                        dve.wait_ge(tap, TAPS.index((j, i - 1)) + 1)
                        nc.vector.scalar_tensor_tensor(conv[:, j, :], glu[:, j, i:i + SEQ], w, conv[:, j, :],
                                                       ALU.mult, ALU.add).then_inc(tap, 1)
                    done_taps[0] = n_tap + 1

            def after(m):
                kind, j = SPLIT[m]
                if kind == "conv":
                    dve.wait_ge(sig_ready, j + 1)
                    nc.vector.tensor_tensor(glu[:, j, CONV_TAPS - 1:], bank[4 + j if j < FIRST else j % 2][:, SEQ:2 * SEQ],
                                            glu_gate[:, j % 2, :], ALU.mult).then_inc(glu_ready, 1)
                    glus[0] += 1

            dve.wait_ge(consts_ready, 1)
            for m in range(SP_AT["v", 0] + 1):
                if m >= 1:
                    after(m - 1)
                if 1 <= m <= SP_AT["v", 1] - 2:
                    split_lo(m + 2)
                if 2 <= m < SP_AT["v", 0]:
                    taps(7 if m < SP_AT["qk", 0] else 10)

            def gn_centre(g):
                dve.wait_ge(gn_mean, g + 1)
                dve.wait_ge(tap, PAIR_TAPS[g])
                dve.wait_ge(pool_tap, (g + 1) * (CONV_TAPS - 1))
                both = conv[:, 2 * g:2 * g + 2, :].rearrange("p a b -> p (a b)")
                nc.vector.tensor_tensor(both, both, bank[GN_BANK[g]][:, :], ALU.subtract).then_inc(gn_centred, 1)

            def gn_scale():
                dve.wait_ge(gn_sq, 2)
                for j in range(CT):
                    dve.wait_ge(gn_bc, j // 2 + 1)
                    half = slice((j % 2) * SEQ, (j % 2) * SEQ + SEQ)
                    nc.vector.scalar_tensor_tensor(conv[:, j, :], conv[:, j, :], col("gn_g", j),
                                                   bank[GN_BANK[j // 2]][:, half], ALU.mult, ALU.mult).then_inc(gn_scaled, 1)

            def mix_parts():
                for j in range(CT):
                    dve.wait_ge(gn_silu, j + 1)
                    nc.vector.tensor_copy(act_hi[:, CT + j, :], xmod[:, CT + j, :]).then_inc(mix_hi, 1)
                for j in range(CT):
                    dve.wait_ge(mix_hi, j + 1)
                    nc.vector.tensor_tensor(act_lo[:, CT + j, :], xmod[:, CT + j, :], act_hi[:, CT + j, :].bitcast(f32),
                                            ALU.subtract).then_inc(mix_lo, 1)

            def qk_normalise(j):
                dve.wait_ge(qk_bc, j + 1)
                dve.wait_ge(qk_raw, j + 1)
                for part, gain in enumerate((q_gain[:, :], col("k_g"))):
                    cut = slice(part * SEQ, (part + 1) * SEQ)
                    nc.vector.scalar_tensor_tensor(qk[:, j, cut], qk[:, j, cut], gain, bank[j % 2][:, cut], ALU.mult,
                                                   ALU.mult).then_inc(qk_normed, 1)

            dve.wait_ge(qk_std, 1)
            nc.vector.reciprocal(qk_inv[:, :], qk_stat[:, :]).then_inc(qk_inverted, 1)
            taps(4)
            dve.wait_ge(qk_turned, 1)
            nc.vector.tensor_copy(qk_rstd[:, :], bank[6][0:16, SEQ:2 * SEQ]).then_inc(qk_rs, 1)
            taps(len(TAPS))
            qk_normalise(0)
            qk_normalise(1)
            dve.wait_ge(mod_done, 1)
            dve.wait_ge(gates_b_ready, 16)
            nc.vector.tensor_tensor(gates_b[:, :], bank[2][:, :], gates_b[:, :], ALU.add).then_inc(mod_rows_ready, 1)
            qk_normalise(2)
            qk_normalise(3)

            def add_bias(h):
                dve.wait_ge(scores, h + 1)
                if h >= 3:
                    dve.wait_ge(turned, h - 2)
                for t, (a, b, c) in enumerate(ROWS):
                    n = 2 * h + t
                    nc.vector.tensor_tensor_reduce(prob[:, h % 3, a:b], bank[h % 2][:, a:b], bias[:, h, SEQ - 1 - c::-1],
                                                   1.0, 2 * NEG, ALU.add, ALU.max, peak[:, n:n + 1]).then_inc(biased, 1)
                dve.wait_ge(biased, 2 * h + 2)
                nc.vector.tensor_scalar(npeak[:, 2 * h:2 * h + 2], peak[:, 2 * h:2 * h + 2], -1.0, None,
                                        ALU.mult).then_inc(peaked, 1)

            def normalise(h):
                dve.wait_ge(exped, 2 * h + 2)
                nc.vector.reciprocal(rtotal[:, 2 * h:2 * h + 2], total[:, 2 * h:2 * h + 2]).then_inc(inverted, 1)
                dve.wait_ge(inverted, h + 1)
                for t, (a, b, _) in enumerate(ROWS):
                    n = 2 * h + t
                    last = nc.vector.tensor_scalar(prob[:, h % 3, a:b], prob[:, h % 3, a:b], rtotal[:, n:n + 1], None,
                                                   ALU.mult)
                last.then_inc(normed, 1)

            def att_lo_part(j):
                dve.wait_ge(att_hi, j + 1)
                nc.vector.tensor_tensor(act_lo[:, j, :], bank[3][:, 0:SEQ], act_hi[:, j, :].bitcast(f32),
                                        ALU.subtract).then_inc(att_lo, 1)

            dve.wait_ge(bias_ready, 16)
            add_bias(0)
            add_bias(1)
            for h in range(HEADS):
                normalise(h)
                if h == 4:
                    gn_scale()
                if h == 0:
                    gn_centre(0)
                    gn_centre(1)
                elif h + 1 < HEADS:
                    add_bias(h + 1)
                if h in (1, 2):
                    dve.wait_ge(gate_bc, h)
                    nc.vector.tensor_copy(gate[:, 0, h * 512 - 512:h * 512], bank[4][:, :]).then_inc(gate_ready, 1)
                if h == 2:
                    dve.wait_ge(gn_std, 1)
                    nc.vector.reciprocal(gn_inv[:, :], gn_stat[:, :]).then_inc(gn_inverted, 1)
                    mod_rows_out()
                elif h == 3:
                    dve.wait_ge(gn_turned, 1)
                    nc.vector.tensor_copy(gn_rstd[:, :], bank[6][0:8, SEQ:2 * SEQ]).then_inc(gn_rs, 1)
                    norm2_columns()
                elif h == 5:
                    mix_parts()
                if h % 2 == 0 and h >= 2:
                    att_lo_part(h // 2 - 1)
                if h in LOW_AT_HEAD:
                    split_lo(LOW_AT_HEAD[h])
            att_lo_part(CT - 1)
            dve.wait_ge(xr_ready, 16)

            def x2_diagonal(t):
                dve.wait_ge(x2_std, t + 1)
                nc.vector.reciprocal(rinv2[:, t:t + 1], rms2[:, t:t + 1]).then_inc(x2_rs, 1)
                dve.wait_ge(x2_rs, t + 1)
                nc.vector.tensor_scalar(diag[:, t, :], ident[:, :], rinv2[:, t:t + 1], None, ALU.mult).then_inc(x2_diag, 1)

            def gated_mixer(i):
                half = slice((i % 2) * 512, (i % 2) * 512 + 512)
                dve.wait_ge(mixed, i + 1)
                nc.vector.tensor_tensor(tmp[:, i, :], bank[OUT_BANK + i][:, :], gate[:, 0, half], ALU.mult).then_inc(x2_part, 1)

            for t in range(ST):
                gated_mixer(2 * t)
                gated_mixer(2 * t + 1)
                if t == 1:
                    x2_diagonal(0)
                dve.wait_ge(x2_part, 2 * t + 2)
                nc.vector.tensor_tensor(xr[:, t, 512:], xr[:, t, 512:], tmp[:, 2 * t + 1, :], ALU.add).then_inc(x2_right, 1)
            dve.wait_ge(x2_right, ST)
            nc.vector.tensor_tensor_reduce(out_rows[:, 2 * ST - 1, :], xr[:, ST - 1, 512:], xr[:, ST - 1, 512:], 1.0, 0.0,
                                           ALU.mult, ALU.add, ssq2[:, 2 * ST - 1:]).then_inc(x2_sq_last, 1)
            x2_diagonal(1)
            for k in range(KT):
                dve.wait_ge(xn2_full, k + 1)
                nc.vector.tensor_copy(act_hi[:, k, :], xt[:, k, :]).then_inc(xn2_hi, 1)
                if k % 2 == 1:
                    dve.wait_ge(xn2_hi, k)
                    nc.vector.tensor_tensor(act_lo[:, k - 1, :], xt[:, k - 1, :], act_hi[:, k - 1, :].bitcast(f32),
                                            ALU.subtract).then_inc(xn2_lo, 1)
            split_lo(SP_AT["up", 1])

            def earlier_taps(t):
                for g in range(2):
                    dve.wait_ge(tap2, 2 * t + g + 1)
                    nc.vector.scalar_tensor_tensor(ug[:, t % 2, g, 1:], bank[4 + 2 * (t % 2) + g][:, 0:SEQ - 1],
                                                   col("ffn_w", (g * FT + t) * FFN_TAPS + 1), ug[:, t % 2, g, 1:],
                                                   ALU.mult, ALU.add).then_inc(tap1, 1)
                for g in range(2):
                    dve.wait_ge(tap1, 2 * t + g + 1)
                    nc.vector.scalar_tensor_tensor(ug[:, t % 2, g, 2:], bank[4 + 2 * (t % 2) + g][:, 0:SEQ - 2],
                                                   col("ffn_w", (g * FT + t) * FFN_TAPS), ug[:, t % 2, g, 2:],
                                                   ALU.mult, ALU.add).then_inc(tap0, 1)

            def gate_hidden(t):
                dve.wait_ge(gated, t + 1)
                if t >= 2:
                    dve.wait_ge(hid_lo_ready, t - 1)
                nc.vector.tensor_tensor(hid[:, t % 2, :], ug[:, t % 2, 0, :], silu_g[:, t % 2, :],
                                        ALU.mult).then_inc(hidden, 1)

            def hid_low(t):
                dve.wait_ge(hid_hi_ready, t + 1)
                if t >= 4:
                    dve.wait_ge(w_used, SP_AT["down", t // 2 - 2] + 1)
                nc.vector.tensor_tensor(hid_lo[:, t % 4, :], hid[:, t % 2, :], hid_hi[:, t % 4, :].bitcast(f32),
                                        ALU.subtract).then_inc(hid_lo_ready, 1)

            m0 = SP_AT["up", 0]
            for m in range(m0, len(SPLIT)):
                done = m > m0 and SPLIT[m - 1][0] == "up"
                if done:
                    earlier_taps(SPLIT[m - 1][1])
                split_lo(m + 2)
                if done:
                    gate_hidden(SPLIT[m - 1][1])
                    hid_low(SPLIT[m - 1][1])
            dve.wait_ge(gate2_ready, 2)
            for i in range(2 * ST - 1):
                half = slice((i % 2) * 512, (i % 2) * 512 + 512)
                dve.wait_ge(down_done, i + 1)
                if i == 2:
                    dve.wait_ge(out_ready, 1)
                nc.vector.tensor_tensor(tmp[:, i % 2, :], bank[i][:, :], gate[:, 1, half], ALU.mult).then_inc(out_part, 1)
                dve.wait_ge(out_part, i + 1)
                nc.vector.tensor_tensor(out_rows[:, i, :], xr[:, i // 2, half], tmp[:, i % 2, :], ALU.add).then_inc(out_ready, 1)
            dve.wait_ge(down_done, 2 * ST)
            dve.wait_ge(out_ready, 2)
            for a in (0, 256):
                nc.vector.tensor_tensor(tmp[:, 1, a:a + 256], bank[2 * ST - 1][:, a:a + 256], gate[:, 1, 512 + a:768 + a],
                                        ALU.mult).then_inc(out_part, 1)
            dve.wait_ge(out_part, 2 * ST + 1)
            nc.vector.tensor_tensor(out_rows[:, 2 * ST - 1, 256:], xr[:, ST - 1, 768:], tmp[:, 1, 256:],
                                    ALU.add).then_inc(out_ready, 1)

        @block.tensor
        def _(pe):
            def product(o, stat, mov, first, last):
                (sh, sl), (mh, ml) = stat, mov
                nc.tensor.matmul(o, sh, mh, start=first, stop=False)
                nc.tensor.matmul(o, sh, ml, start=False, stop=False)
                return nc.tensor.matmul(o, sl, mh, start=False, stop=last)

            def weights(m, a, n):
                hi, lo = parts(m)
                return hi[:, a:a + n], lo[:, a:a + n]

            def acts(k, a, n):
                return act_hi[:, k, a:a + n], act_lo[:, k, a:a + n]

            def ready(m):
                pe.wait_ge(lo_done, m + 1)
                pe.wait_ge(hi_done, m + 1)

            def ada(n, to):
                arrived(pe, "ada", n)
                k = n % KT
                for q in range(4):
                    last = nc.tensor.matmul(bank[to][32 * q:32 * q + 32, :], silu_c[:, k:k + 1].to_broadcast([P, 32]),
                                            slot("ada", n)[:, 512 * q:512 * q + 512], start=(k == 0), stop=(k == KT - 1))
                last.then_inc(ada_used, 1)

            def ada_end(groups):
                pe.wait_ge(ada_used, groups * KT)
                nc.tensor.transpose(bank[7 if groups == 2 else 5][:, SEQ:SEQ + P], ident[:, :], ident[:, :]).then_inc(mod_done, 1)

            def turn_mod_rows(to):
                for j in range(4):
                    last = nc.tensor.transpose(bank[to][:, j * P:(j + 1) * P], mod_rows[:, j * P:(j + 1) * P], ident[:, :])
                last.then_inc(mod_cols_ready, 1)

            def keep_clock(n, to):
                for _ in range(n):
                    nc.tensor.transpose(bank[to][:, 0:P], ident[:, :], ident[:, :])

            pe.wait_ge(consts_ready, 1)
            pe.wait_ge(xsq_ready, 1)
            for k in range(KT):
                last = nc.tensor.matmul(bank[7][:, 0:SEQ], ones[:, :], xmod[:, k, :], start=(k == 0), stop=(k == KT - 1))
            last.then_inc(ssq_ready, 1)

            def ada_rows(k):
                arrived(pe, "ada", k)
                if k >= 2:
                    pe.wait_ge(norm1_copied, k - 1)
                for i in range(2):
                    for q in range(4):
                        kk = 2 * q + i
                        last = nc.tensor.matmul(bank[2 + k % 2][32 * q:32 * q + 32, 0:2 * P],
                                                silu_c[:, kk:kk + 1].to_broadcast([P, 32]),
                                                slot("ada", k)[:, 2 * P * kk:2 * P * (kk + 1)], start=(i == 0), stop=(i == 1))
                last.then_inc(ada_used, 1)

            def ada_columns(k):
                pe.wait_ge(norm1_copied, k + 1)
                if k == 1:
                    pe.wait_ge(rms_ready, 1)
                if k >= 2:
                    pe.wait_ge(norm1_read, k - 1)
                for g in range(2):
                    a = (2 * (k % 2) + g) * P
                    last = nc.tensor.matmul(bank[6 + k % 2][:, 2 * k + g:2 * k + g + 1], mod_rows[:, a:a + P], pick[:, :],
                                            start=True, stop=True)
                last.then_inc(norm1_turned, 1)

            def first_products(k):
                pe.wait_ge(xn_hi, k + 1)
                if k < POOL_LOWS:
                    pe.wait_ge(xn_lo_pool, k + 1)
                else:
                    pe.wait_ge(xn_lo, k - POOL_LOWS + 1)
                for m in range(FIRST):
                    if k == 0:
                        ready(m)
                    for c in range(2):
                        last = product(bank[m + 4 * c][:, c * SEQ:(c + 1) * SEQ], weights(m, k * 2 * P + c * P, P),
                                       acts(k, 0, SEQ), k == 0, k == KT - 1)
                    if k == KT - 1:
                        last.then_inc(w_used, 1)

            pe.wait_ge(silu_c_ready, 1)
            for k in range(KT):
                ada_rows(k)
                if k >= 1:
                    ada_columns(k - 1)
                if k == 2:
                    keep_clock(30, 3)
                for tile in PRODUCTS_AFTER.get(k, ()):
                    first_products(tile)
            ada_columns(KT - 1)
            for tile in PRODUCTS_AFTER[KT]:
                first_products(tile)

            def pair(m, to):
                for c in range(2):
                    for k in range(KT):
                        last = product(bank[to][:, c * SEQ:(c + 1) * SEQ], weights(m, k * 2 * P + c * P, P),
                                       acts(k, 0, SEQ), k == 0, k == KT - 1)
                last.then_inc(w_used, 1)

            ada_at = [KT]

            def later_ada(after):
                for _ in range(ADA_AFTER.get(after, 0)):
                    ada(ada_at[0], 2)
                    ada_at[0] += 1

            for j in range(FIRST, CT):
                m = SP_AT["conv", j]
                ready(m)
                pe.wait_ge(glu_ready, j - 1)
                pair(m, j % 2)
                later_ada(("conv", j))

            def qk_squares(j):
                pe.wait_ge(qk_sq_ready, j + 1)
                for t in range(ST):
                    for part in range(2):
                        a = t * 16 + part * 8 + 2 * j
                        last = nc.tensor.matmul(bank[6][:, a:a + 2],
                                                qk_sq[:, j % 2, part * SEQ + t * P:part * SEQ + (t + 1) * P],
                                                to_group[:, 0, 0:2], start=True, stop=True)
                last.then_inc(qk_ssq, 1)

            def qk_turn():
                pe.wait_ge(qk_inverted, 1)
                for t in range(ST):
                    last = nc.tensor.transpose(bank[6][0:16, SEQ + t * P:SEQ + (t + 1) * P],
                                               qk_inv[:, t * 16:(t + 1) * 16], ident[:, :])
                last.then_inc(qk_turned, 1)

            for j in range(CT):
                m = SP_AT["qk", j]
                ready(m)
                if j < 2:
                    pe.wait_ge(glu_ready, CT - 1 + j)
                else:
                    pe.wait_ge(qk_sq_ready, j - 1)
                pair(m, j % 2)
                if j >= 1:
                    qk_squares(j - 1)
                later_ada(("qk", j))

            def qk_spread(j):
                pe.wait_ge(qk_rs, 1)
                if j >= 2:
                    pe.wait_ge(qk_normed, 2 * (j - 1))
                else:
                    pe.wait_ge(qk_sq_ready, CT)
                for part in range(2):
                    last = nc.tensor.matmul(bank[j % 2][:, part * SEQ:(part + 1) * SEQ], from_group[:, 4 * part + j, :],
                                            qk_rstd[:, :], start=True, stop=True)
                last.then_inc(qk_bc, 1)

            def gn_means(g):
                pe.wait_ge(tap, PAIR_TAPS[g])
                pe.wait_ge(pool_tap, (g + 1) * (CONV_TAPS - 1))
                for c in range(2):
                    last = nc.tensor.matmul(bank[GN_BANK[g]][:, c * SEQ:(c + 1) * SEQ], half_mean[:, :],
                                            conv[:, 2 * g + c, :], start=True, stop=True)
                last.then_inc(gn_mean, 1)

            def gn_squares():
                for c in range(CT):
                    pe.wait_ge(gn_sq, c // 2 + 1)
                    for t in range(ST):
                        a = t * 8 + 2 * c
                        last = nc.tensor.matmul(bank[6][:, a:a + 2], xmod[:, c, t * P:(t + 1) * P],
                                                to_group[:, 0, 0:2], start=True, stop=True)
                last.then_inc(gn_ssq, 1)

            def gn_turn():
                pe.wait_ge(gn_inverted, 1)
                for t in range(ST):
                    last = nc.tensor.transpose(bank[6][0:8, SEQ + t * P:SEQ + (t + 1) * P], gn_inv[:, t * 8:(t + 1) * 8],
                                               ident[:, :])
                last.then_inc(gn_turned, 1)

            def gn_spread():
                pe.wait_ge(gn_rs, 1)
                for c in range(CT):
                    last = nc.tensor.matmul(bank[GN_BANK[c // 2]][:, (c % 2) * SEQ:(c % 2) * SEQ + SEQ],
                                            from_group[0:8, c, :], gn_rstd[:, :], start=True, stop=True)
                    if c % 2 == 1:
                        last.then_inc(gn_bc, 1)

            def v_half(i, t):
                m = SP_AT["v", i]
                ready(m)
                for k in range(KT // 2):
                    kk = i * KT // 2 + k
                    last = product(bank[4 + t][:, :], acts(kk, t * P, P), weights(m, k * 512, 512),
                                   kk == 0, kk == KT - 1)
                return last

            def late_ada(n):
                for _ in range(n):
                    ada(ada_at[0], 2 if ada_at[0] < 2 * KT else 7)
                    ada_at[0] += 1
                    if ada_at[0] == 2 * KT:
                        ada_end(2)

            v_half(0, 0)
            qk_squares(CT - 1)
            v_half(0, 1).then_inc(w_used, 1)
            qk_turn()
            if ada_at[0] == 2 * KT:
                ada_end(2)
            late_ada(3)
            qk_spread(0)
            qk_spread(1)
            v_half(1, 0)
            late_ada(1)
            qk_spread(2)
            qk_spread(3)
            v_half(1, 1).then_inc(w_used, 1)

            def head_scores(h):
                j, r = h // 2, slice(64 * (h % 2), 64 * (h % 2) + 64)
                pe.wait_ge(qk_normed, max(2 * (j + 1), 2 * CT if h < 2 else 0))
                if h >= 2:
                    pe.wait_ge(biased, 2 * (h - 1))
                for t, (a, b, _) in enumerate(ROWS):
                    last = nc.tensor.matmul(bank[h % 2][:, a:b], qk[r, j, t * P:(t + 1) * P], qk[r, j, SEQ:SEQ + b - a],
                                            start=True, stop=True)
                last.then_inc(scores, 1)

            def head_turn(h):
                pe.wait_ge(normed, h + 1)
                if h >= 1:
                    pe.wait_ge(turned_copied, h)
                for t in range(3):
                    last = nc.tensor.transpose(bank[2][:, t * P:(t + 1) * P], prob[:, h % 3, t * P:(t + 1) * P],
                                               ident[:, :])
                last.then_inc(turned, 1)

            def head_values(h):
                pe.wait_ge(turned_copied, h + 1)
                r = slice(64 * (h % 2), 64 * (h % 2) + 64)
                if h % 2 == 0 and h >= 2:
                    pe.wait_ge(att_lo, h // 2)
                nc.tensor.matmul(bank[3][r, 0:SEQ], v[:, 0, h * 64:(h + 1) * 64], prob_t[:, h % 2, 0:SEQ],
                                 start=True, stop=False)
                nc.tensor.matmul(bank[3][r, P:SEQ], v[:, 1, h * 64:(h + 1) * 64], prob_t[:, h % 2, SEQ:384],
                                 start=False, stop=True).then_inc(attended, 1)

            def spread_gate(n):
                nc.tensor.matmul(bank[4 if n < 2 else 2 + n][:, :], ones[32 * n:32 * n + 1, :],
                                 gates_b[32 * n:32 * n + 1, :], start=True, stop=True,
                                 tile_position=(32 * n, 0)).then_inc(gate_bc, 1)

            def out_part(i, banks=range(2 * ST)):
                m, k = SP_AT["out", i // 2], OUT_TILES[i]
                ready(m)
                if k >= CT:
                    pe.wait_ge(mix_lo, k - CT + 1)
                else:
                    pe.wait_ge(att_lo, k + 1)
                for b in banks:
                    t, n = b // 2, b % 2
                    last = product(bank[OUT_BANK + b][:, :], acts(k, t * P, P),
                                   weights(m, (i % 2) * D_MODEL + n * 512, 512), i == 0, i == KT - 1)
                return last

            head_scores(0)
            head_scores(1)
            gn_means(0)
            pe.wait_ge(v_ready, ST)
            gn_means(1)
            for h in range(HEADS):
                if 1 < h + 1 < HEADS:
                    head_scores(h + 1)
                head_turn(h)
                if h == 0:
                    spread_gate(0)
                elif h == 1:
                    gn_squares()
                elif h == 2:
                    pe.wait_ge(gate_ready, 1)
                    spread_gate(1)
                elif h == 3:
                    pe.wait_ge(mod_rows_ready, 2)
                    pe.wait_ge(gate_ready, 2)
                    turn_mod_rows(4)
                    keep_clock(7, 5)
                    gn_spread()
                elif h == 4:
                    pe.wait_ge(mod_cols_read, 2)
                    out_part(0, [0, 3])
                    pe.wait_ge(gn_scaled, CT)
                    out_part(0, [1, 2])
                elif h == 5:
                    out_part(1).then_inc(w_used, 1)
                    out_part(2)
                elif h == 6:
                    out_part(3).then_inc(w_used, 1)
                    out_part(4)
                else:
                    out_part(5).then_inc(w_used, 1)
                if h < len(ADA_AT_HEAD):
                    late_ada(ADA_AT_HEAD[h])
                    if h == len(ADA_AT_HEAD) - 1:
                        ada_end(3)
                head_values(h)
                if h == 2:
                    gn_turn()
            for t in range(ST):
                out_part(6, [2 * t, 2 * t + 1])
                for b in (2 * t, 2 * t + 1):
                    out_part(7, [b]).then_inc(mixed, 1)
            nc.tensor.transpose(bank[3][:, 0:P], ident[:, :], ident[:, :]).then_inc(w_used, 1)
            for n in range(2):
                pe.wait_ge(x2_part, n + 1)
                spread_gate(2 + n)
            pe.wait_ge(biased, 2 * HEADS)
            pe.wait_ge(att_lo, CT)
            for t in range(ST):
                pe.wait_ge(x2_diag, t + 1)
                pe.wait_ge(x2_left, t + 1)
                pe.wait_ge(x2_right, t + 1)
                for k in range(KT):
                    last = nc.tensor.matmul(bank[k // 2][:, (k % 2) * SEQ + t * P:(k % 2) * SEQ + (t + 1) * P],
                                            xr[:, t, k * P:(k + 1) * P], diag[:, t, :], start=True, stop=True)
                    if t == ST - 1:
                        last.then_inc(x2_turned, 1)

            def up(t):
                m = SP_AT["up", t]
                ready(m)
                if t == 0:
                    pe.wait_ge(gate2_ready, 2)
                elif t == 1:
                    pe.wait_ge(x2_part, 2 * ST)
                if t >= 2:
                    pe.wait_ge(tap0, 2 * (t - 1))
                for g in range(2):
                    for k in range(KT):
                        if t == 0 and g == 0:
                            pe.wait_ge(xn2_lo_pool if k % 2 else xn2_lo, k // 2 + 1)
                        last = product(bank[4 + 2 * (t % 2) + g][:, 0:SEQ], weights(m, k * 2 * P + g * P, P),
                                       acts(k, 0, SEQ), k == 0, k == KT - 1)
                last.then_inc(w_used, 1)

            def down(i):
                m = SP_AT["down", i]
                ready(m)
                pe.wait_ge(hid_lo_ready, 2 * i + 2)
                pe.wait_ge(hid_hi_ready, 2 * i + 2)
                order = [(f, b) for f in range(2) for b in range(2 * ST)] if i < FT // 2 - 1 else \
                        [(f, b) for b in range(2 * ST) for f in range(2)]
                for f, b in order:
                    t, n = b // 2, b % 2
                    place = (2 * i + f) % 4
                    h = (hid_hi[:, place, t * P:(t + 1) * P], hid_lo[:, place, t * P:(t + 1) * P])
                    last = product(bank[b][:, :], h, weights(m, f * D_MODEL + n * 512, 512),
                                   i == 0 and f == 0, i == FT // 2 - 1 and f == 1)
                    if i == FT // 2 - 1 and f == 1:
                        last.then_inc(down_done, 1)
                if i < FT // 2 - 1:
                    last.then_inc(w_used, 1)

            for kind, i in UP_DOWN:
                (up if kind == "up" else down)(i)


def _layout(x, c, rel_bias, ada_w, ada_b, norm1_g, w_in, q_norm_g, k_norm_g, conv_dw_w, conv_dw_b, conv_norm_g,
            conv_norm_b, w_out, norm2_g, w_up, ffn_dw_w, ffn_dw_b, w_down):
    a = {k: np.asarray(v) for k, v in locals().items()}

    def by_tile(v):
        return v.reshape(-1, P).T

    def pairs(w, first, second, n):
        w = w.reshape(KT, P, -1, P)
        return [np.stack([w[:, :, first + j], w[:, :, second + j]], 2).transpose(1, 0, 2, 3).reshape(P, SLOT)
                for j in range(n)]

    ada = a["ada_w"][0].reshape(KT, P, 12, 512)
    w_in = a["w_in"][0]
    slots = {}
    first = a["ada_w"][0].reshape(KT, P, 6, KT, P)[:, :, 0:2]
    for k in range(KT):
        slots["ada", k] = first[:, :, :, k].transpose(1, 0, 2, 3).reshape(P, SLOT)
    for g, chunks in list(enumerate(ADA_GROUPS))[1:]:
        for k in range(KT):
            slots["ada", g * KT + k] = ada[k][:, list(chunks)].reshape(P, SLOT)
    for j, s in enumerate(pairs(w_in, 16, 12, CT)):
        slots["conv", j] = s
    for j, s in enumerate(pairs(w_in, 0, 4, CT)):
        slots["qk", j] = s
    wv = w_in[:, 1024:1536].reshape(2, KT // 2, P, 512)
    for i in range(2):
        slots["v", i] = wv[i].transpose(1, 0, 2).reshape(P, SLOT)
    wo = a["w_out"][0].reshape(KT, P, D_MODEL).transpose(1, 0, 2)
    for j in range(4):
        slots["out", j] = wo[:, OUT_TILES[2 * j:2 * j + 2]].reshape(P, SLOT)
    for t, s in enumerate(pairs(a["w_up"][0], 0, FT, FT)):
        slots["up", t] = s
    wd = a["w_down"][0].reshape(FT // 2, 2, P, D_MODEL)
    for i in range(FT // 2):
        slots["down", i] = wd[i].transpose(1, 0, 2).reshape(P, SLOT)
    stream = np.stack([slots[s] for s in STREAM])

    b = a["ada_b"][0].reshape(6, D_MODEL)
    parts = {
        "c": by_tile(a["c"][0]), "norm1_g": by_tile(a["norm1_g"][0]), "norm2_g": by_tile(a["norm2_g"][0]),
        "sh1_b": by_tile(b[0]), "sc1_b": by_tile(b[1]), "sh2_b": by_tile(b[3]), "sc2_b": by_tile(b[4]),
        "conv_w": a["conv_dw_w"][0].reshape(CONV_TAPS, CT, P).transpose(2, 1, 0).reshape(P, -1),
        "conv_b": by_tile(a["conv_dw_b"][0]), "gn_g": by_tile(a["conv_norm_g"][0]), "gn_b": by_tile(a["conv_norm_b"][0]),
        "ffn_w": a["ffn_dw_w"][0].reshape(FFN_TAPS, 2 * FT, P).transpose(2, 1, 0).reshape(P, -1),
        "ffn_b": by_tile(a["ffn_dw_b"][0]),
        "q_g": np.tile(a["q_norm_g"][0], 2)[:, None], "k_g": np.tile(a["k_norm_g"][0], 2)[:, None],
    }
    cols = np.concatenate([parts[k] for k in COLS], axis=1)
    x2 = a["x"][0]
    return {
        "stream": stream,
        "x_t": x2.T.reshape(KT, P, SEQ).transpose(1, 0, 2),
        "x_rows": x2.reshape(ST, P, D_MODEL).transpose(1, 0, 2),
        "cols": cols,
        "ada_b_gates": np.repeat(a["ada_b"][0].reshape(12, 512)[list(ADA_GROUPS[1])], 32, axis=0),
        "rel_bias": a["rel_bias"],
    }


def kernel(**inputs):
    import concourse.bacc as _bacc
    from concourse.bass_utils import run_bass_kernel_spmd as _run

    nc = _bacc.Bacc("TRN2", target_bir_lowering=False, num_devices=1)
    arrays, args = {}, []
    for name, a in _layout(**inputs).items():
        a = np.ascontiguousarray(a)
        arrays[f"in_{name}"] = a
        args.append(nc.dram_tensor(f"in_{name}", a.shape, mybir.dt.from_np(a.dtype), kind="ExternalInput").ap())
    out = nc.dram_tensor("out_0", (ST, P, D_MODEL), mybir.dt.float32, kind="ExternalOutput").ap()
    hymba_layer(nc, *args, out)
    r = _run(nc, [arrays], core_ids=[0])
    return r.results[0]["out_0"].reshape(1, SEQ, D_MODEL)
```
